# Optimizing a Trainium2 kernel written in Bass

```python
import jax, jax.numpy as jnp
from jax import lax
import numpy as np

D_MODEL = 1024
BATCH = 1
SEQ = 1024
DEPTH = 1

GRID_W = 64
CTX_LEN = 256
D_MIX = 1024
D_FOURIER = 256
N_FOURIER_GROUPS = 4
FOURIER_GROUP = D_FOURIER // N_FOURIER_GROUPS
HEAD_DIM = 64
N_NA_HEADS = 12
D_NA = N_NA_HEADS * HEAD_DIM
NA_ROWS_MAX = 8
NA_COLS = 16
ROPE_THETA = 10000.0
N_GROUPS = 4
EXPERTS_PER_GROUP = 8
N_EXPERTS = N_GROUPS * EXPERTS_PER_GROUP
TOP_K = 2
D_EXPERT = 512
MOE_BLOCK = 128
N_MOD = 6
D_IN_PROJ = D_FOURIER + 3 * D_NA
EPS = 1e-6

kernel_name = "hymba_fnet_natten_hmoe_dit"

def rmsnorm(x, g):
    xf = x.astype(jnp.float32)
    r = lax.rsqrt(jnp.mean(xf * xf, axis=-1, keepdims=True) + EPS)
    return (xf * r * g.astype(jnp.float32)).astype(x.dtype)

def adaln(cond, w, b):
    mod = jax.nn.silu(cond) @ w + b
    return [m[:, None, :] for m in jnp.split(mod, N_MOD, axis=-1)]

def modulate(h, shift, scale):
    return h * (1.0 + scale) + shift

def fourier_mix(f, w_fmix):
    b, n, _ = f.shape
    fg = f.astype(jnp.float32).reshape(b, n, N_FOURIER_GROUPS, FOURIER_GROUP)
    fr = jnp.fft.fft2(fg, axes=(1, 3), norm="ortho").real
    return fr.reshape(b, n, D_FOURIER).astype(f.dtype) @ w_fmix

def _rotate(x, pos):
    half = x.shape[-1] // 2
    inv = ROPE_THETA ** (-jnp.arange(half, dtype=jnp.float32) / half)
    ang = pos.astype(jnp.float32)[:, None] * inv[None, :]
    cos = jnp.cos(ang)[None, :, None, :]
    sin = jnp.sin(ang)[None, :, None, :]
    x1, x2 = x[..., :half], x[..., half:]
    return jnp.concatenate([x1 * cos - x2 * sin, x1 * sin + x2 * cos], axis=-1)

def axial_rope(x):
    n = x.shape[1]
    t = jnp.arange(n)
    row, col = t // GRID_W, t % GRID_W
    xf = x.astype(jnp.float32)
    r = HEAD_DIM // 2
    out = jnp.concatenate([_rotate(xf[..., :r], row), _rotate(xf[..., r:], col)], axis=-1)
    return out.astype(x.dtype)

def neighbourhood_attention(q, k, v, k_ctx, v_ctx, rpb):
    b, n, h, hd = q.shape
    rows = n // GRID_W
    ks_r = min(NA_ROWS_MAX, rows)
    scale = HEAD_DIM ** -0.5
    qr = axial_rope(q).reshape(b, rows, GRID_W, h, hd)
    kg = axial_rope(k).reshape(b, rows, GRID_W, h, hd)
    vg = v.reshape(b, rows, GRID_W, h, hd)
    qp = q.reshape(b, rows, GRID_W, h, hd)
    r = jnp.arange(rows)
    row_start = jnp.clip(r - ks_r // 2, 0, rows - ks_r)
    row_idx = row_start[:, None] + jnp.arange(ks_r)[None, :]
    k_blk = kg[:, row_idx]
    v_blk = vg[:, row_idx]
    s_loc = jnp.einsum('brqhd,brkwhd->bhrqkw', qr, k_blk,
                       preferred_element_type=jnp.float32) * scale
    cidx = jnp.arange(GRID_W)
    col_start = jnp.clip(cidx - NA_COLS // 2, 0, GRID_W - NA_COLS)
    col_valid = (cidx[None, :] >= col_start[:, None]) & (cidx[None, :] < col_start[:, None] + NA_COLS)
    dr = row_idx - r[:, None] + (NA_ROWS_MAX - 1)
    dc = jnp.clip(cidx[None, :] - cidx[:, None] + (NA_COLS - 1), 0, 2 * NA_COLS - 2)
    bias = rpb[:, dr[:, None, :, None], dc[None, :, None, :]]
    s_loc = s_loc + bias[None].astype(jnp.float32)
    s_loc = jnp.where(col_valid[None, None, None, :, None, :], s_loc, jnp.finfo(jnp.float32).min)
    s_loc = s_loc.reshape(b, h, rows, GRID_W, ks_r * GRID_W)
    s_ctx = jnp.einsum('brqhd,blhd->bhrql', qp, k_ctx,
                       preferred_element_type=jnp.float32) * scale
    p = jax.nn.softmax(jnp.concatenate([s_loc, s_ctx], axis=-1), axis=-1)
    n_loc = ks_r * GRID_W
    p_loc = p[..., :n_loc].reshape(b, h, rows, GRID_W, ks_r, GRID_W).astype(v.dtype)
    p_ctx = p[..., n_loc:].astype(v.dtype)
    out = (jnp.einsum('bhrqkw,brkwhd->brqhd', p_loc, v_blk)
           + jnp.einsum('bhrql,blhd->brqhd', p_ctx, v_ctx))
    return out.reshape(b, n, h * hd)

def context_attention(q, k, v):
    b, l, h, hd = q.shape
    s = jnp.einsum('blhd,bmhd->bhlm', q, k, preferred_element_type=jnp.float32) * (HEAD_DIM ** -0.5)
    p = jax.nn.softmax(s, axis=-1).astype(v.dtype)
    return jnp.einsum('bhlm,bmhd->blhd', p, v).reshape(b, l, h * hd)

def hierarchical_moe(h2, w_rg, w_re, w_gate, w_up, w_down):
    n, d = h2.shape
    lg = (h2 @ w_rg).astype(jnp.float32)
    pg = jax.nn.softmax(lg, axis=-1)
    g_sel = jnp.argmax(lg, axis=-1)
    le = (h2 @ w_re).astype(jnp.float32).reshape(n, N_GROUPS, EXPERTS_PER_GROUP)
    le_sel = jnp.take_along_axis(le, g_sel[:, None, None], axis=1)[:, 0]
    pe = jax.nn.softmax(le_sel, axis=-1)
    top_w, top_i = lax.top_k(pe, TOP_K)
    top_w = top_w / jnp.sum(top_w, axis=-1, keepdims=True)
    gate = top_w * jnp.take_along_axis(pg, g_sel[:, None], axis=1)
    eid = g_sel[:, None] * EXPERTS_PER_GROUP + top_i
    m = n * TOP_K
    e_flat = eid.reshape(-1)
    tok_flat = jnp.repeat(jnp.arange(n, dtype=jnp.int32), TOP_K)
    gate_flat = gate.reshape(-1)
    order = jnp.argsort(e_flat)
    e_s, tok_s, gate_s = e_flat[order], tok_flat[order], gate_flat[order]
    counts = jnp.bincount(e_flat, length=N_EXPERTS)
    starts = jnp.cumsum(counts) - counts
    pcounts = ((counts + MOE_BLOCK - 1) // MOE_BLOCK) * MOE_BLOCK
    pends = jnp.cumsum(pcounts)
    pstarts = pends - pcounts
    dest = pstarts[e_s] + (jnp.arange(m) - starts[e_s])
    n_blocks = -(-m // MOE_BLOCK) + N_EXPERTS
    p_slots = n_blocks * MOE_BLOCK
    slot_tok = jnp.zeros((p_slots,), jnp.int32).at[dest].set(tok_s)
    slot_gate = jnp.zeros((p_slots,), jnp.float32).at[dest].set(gate_s)
    block_expert = jnp.minimum(
        jnp.searchsorted(pends, jnp.arange(n_blocks) * MOE_BLOCK, side='right'), N_EXPERTS - 1)
    xs = h2[slot_tok].reshape(n_blocks, MOE_BLOCK, d)

    def expert_block(args):
        xb, e = args
        return (jax.nn.silu(xb @ w_gate[e]) * (xb @ w_up[e])) @ w_down[e]

    ys = lax.map(expert_block, (xs, block_expert)).reshape(p_slots, d)
    ys = ys * slot_gate[:, None].astype(ys.dtype)
    return jnp.zeros((n, d), h2.dtype).at[slot_tok].add(ys)

def setup_inputs(seed: int = 0) -> dict:
    key = jax.random.key(seed)
    ks = jax.random.split(key, 20)
    f32 = jnp.float32
    nrm = lambda k, shape, s: jax.random.normal(k, shape, f32) * s
    return {
        "x": nrm(ks[0], (BATCH, SEQ, D_MODEL), 1.0),
        "c": nrm(ks[1], (BATCH, D_MODEL), 1.0),
        "ctx": nrm(ks[2], (BATCH, CTX_LEN, D_MODEL), 1.0),
        "c_ctx": nrm(ks[3], (D_MODEL,), 1.0),
        "w_ada": nrm(ks[4], (DEPTH, D_MODEL, N_MOD * D_MODEL), 0.5 * D_MODEL ** -0.5),
        "b_ada": nrm(ks[5], (DEPTH, N_MOD * D_MODEL), 0.02),
        "g_norm1": 1.0 + nrm(ks[6], (DEPTH, D_MODEL), 0.05),
        "w_in": nrm(ks[7], (DEPTH, D_MODEL, D_IN_PROJ), D_MODEL ** -0.5),
        "w_fmix": nrm(ks[8], (DEPTH, D_FOURIER, D_FOURIER), D_FOURIER ** -0.5),
        "rpb": nrm(ks[9], (DEPTH, N_NA_HEADS, 2 * NA_ROWS_MAX - 1, 2 * NA_COLS - 1), 0.2),
        "g_out": 1.0 + nrm(ks[10], (DEPTH, D_MIX), 0.05),
        "w_out": nrm(ks[11], (DEPTH, D_MIX, D_MODEL), D_MIX ** -0.5),
        "g_norm2": 1.0 + nrm(ks[12], (DEPTH, D_MODEL), 0.05),
        "w_router_group": nrm(ks[13], (DEPTH, D_MODEL, N_GROUPS), D_MODEL ** -0.5),
        "w_router_expert": nrm(ks[14], (DEPTH, D_MODEL, N_EXPERTS), D_MODEL ** -0.5),
        "w_gate": nrm(ks[15], (DEPTH, N_EXPERTS, D_MODEL, D_EXPERT), D_MODEL ** -0.5),
        "w_up": nrm(ks[16], (DEPTH, N_EXPERTS, D_MODEL, D_EXPERT), D_MODEL ** -0.5),
        "w_down": nrm(ks[17], (DEPTH, N_EXPERTS, D_EXPERT, D_MODEL), D_EXPERT ** -0.5),
        "g_final": 1.0 + nrm(ks[18], (D_MODEL,), 0.05),
    }

def reference(x, c, ctx, c_ctx, w_ada, b_ada, g_norm1, w_in, w_fmix, rpb, g_out, w_out, g_norm2,
              w_router_group, w_router_expert, w_gate, w_up, w_down, g_final):
    b, n, d = x.shape
    l = ctx.shape[1]
    xc = ctx
    q_end = D_FOURIER + D_NA
    k_end = D_FOURIER + 2 * D_NA
    for i in range(DEPTH):
        last = i == DEPTH - 1
        sh1, sc1, gt1, sh2, sc2, gt2 = adaln(c, w_ada[i], b_ada[i])
        csh1, csc1, cgt1, csh2, csc2, cgt2 = adaln(c_ctx[None, :], w_ada[i], b_ada[i])

        h = modulate(rmsnorm(x, g_norm1[i]), sh1, sc1)
        hc = modulate(rmsnorm(xc, g_norm1[i]), csh1, csc1)
        p = h @ w_in[i]
        pc = hc @ w_in[i]
        q = p[..., D_FOURIER:q_end].reshape(b, n, N_NA_HEADS, HEAD_DIM)
        k = p[..., q_end:k_end].reshape(b, n, N_NA_HEADS, HEAD_DIM)
        v = p[..., k_end:].reshape(b, n, N_NA_HEADS, HEAD_DIM)
        kc = pc[..., q_end:k_end].reshape(b, l, N_NA_HEADS, HEAD_DIM)
        vc = pc[..., k_end:].reshape(b, l, N_NA_HEADS, HEAD_DIM)
        f_out = fourier_mix(p[..., :D_FOURIER], w_fmix[i])
        na_out = neighbourhood_attention(q, k, v, kc, vc, rpb[i])
        y = jnp.concatenate([rmsnorm(f_out, g_out[i][:D_FOURIER]),
                             rmsnorm(na_out, g_out[i][D_FOURIER:])], axis=-1) @ w_out[i]
        x = x + gt1 * y
        if not last:
            qc = pc[..., D_FOURIER:q_end].reshape(b, l, N_NA_HEADS, HEAD_DIM)
            fc_out = fourier_mix(pc[..., :D_FOURIER], w_fmix[i])
            nac_out = context_attention(qc, kc, vc)
            yc = jnp.concatenate([rmsnorm(fc_out, g_out[i][:D_FOURIER]),
                                  rmsnorm(nac_out, g_out[i][D_FOURIER:])], axis=-1) @ w_out[i]
            xc = xc + cgt1 * yc

        h2 = modulate(rmsnorm(x, g_norm2[i]), sh2, sc2)
        moe = hierarchical_moe(h2.reshape(b * n, d), w_router_group[i], w_router_expert[i],
                               w_gate[i], w_up[i], w_down[i]).reshape(b, n, d)
        x = x + gt2 * moe
        if not last:
            h2c = modulate(rmsnorm(xc, g_norm2[i]), csh2, csc2)
            moec = hierarchical_moe(h2c.reshape(b * l, d), w_router_group[i], w_router_expert[i],
                                    w_gate[i], w_up[i], w_down[i]).reshape(b, l, d)
            xc = xc + cgt2 * moec
    return rmsnorm(x, g_final)


_drawn_inputs = setup_inputs


def setup_inputs(seed=0):
    import zlib

    import numpy as np

    out = dict(_drawn_inputs(seed))
    spreads = {}
    factors = {'g_norm1': 3.441, 'rpb': 3.594, 'g_out': 3.268, 'g_norm2': 2.883}
    for name, (base, spread) in spreads.items():
        noise = np.random.default_rng([zlib.crc32(name.encode()), seed]).standard_normal(out[name].shape)
        drawn = base * np.exp(spread * noise) if base else spread * noise
        out[name] = __import__('jax').numpy.asarray(drawn.astype(out[name].dtype))
    for name, factor in factors.items():
        out[name] = (out[name] * factor).astype(out[name].dtype)
    return out
```

```python
from contextlib import ExitStack

import numpy as np

import concourse.bass as bass
from concourse import mybir

F32 = mybir.dt.float32
BF16 = mybir.dt.bfloat16
I32 = mybir.dt.int32
ALU = mybir.AluOpType
ACT = mybir.ActivationFunctionType
AX = mybir.AxisListType

P = 128
D = 1024
KD = D // P
N = 1024
NT = N // P
L = 256
GW = 64
HD = 64
NH = 12
HP = NH // 2
DF = 256
DN = NH * HD
NG = 4
NE = 32
EPG = NE // NG
DE = 512
KE = DE // P
EPS = 1e-6

QR, QC, KR, KC = 8, 16, 12, 32
LOC = KR * KC
KEYS = LOC + L
COL0 = [0, 8, 24, 32]
KIND = [0, 1, 1, 2]
PITCH = 32
LEAD = 144
RPB = 768
NEG = -1.0e30
LOWEST = -3.0e38

START = 1
CAP = P
OVB = 16
SLOTS = (NE + OVB) * CAP
SKIP = 1 << 20


class Counter:

    def __init__(self, engine, sem, base=0):
        self.engine, self.sem, self.base, self.n = engine, sem, base, 0

    def step(self, instruction):
        instruction.then_inc(self.sem, 1)
        self.n += 1
        self.engine.wait_ge(self.sem, self.base + self.n)


class Buffers:
    pass


class Arrays:

    def __init__(self, d):
        self.vecs, self.b_ada, self.w_ada, self.x_nat, self.x_perm, self.ctx = d["vecs"], d["b_ada"], d["w_ada"], d["x_nat"], d["x_perm"], d["ctx"]
        self.w_in, self.w_fmix, self.w_out, self.w_router, self.rpb = d["w_in"], d["w_fmix"], d["w_out"], d["w_router"], d["rpb"]
        self.w_gate, self.w_up, self.w_down, self.g_final = d["w_gate"], d["w_up"], d["w_down"], d["g_final"]
        self.ident, self.eye16, self.chan, self.dft, self.rope, self.rot, self.mask = (
            d["ident"], d["eye16"], d["chan"], d["dft"], d["rope"], d["rot"], d["mask"])
        self.before, self.desc, self.base, self.blk, self.ids = d["before"], d["desc"], d["base"], d["blk"], d["ids"]


class Mem:

    def __init__(self, nc, stack):
        self.nc, self.stack = nc, stack

    def sb(self, name, shape, dt=F32):
        return self.stack.enter_context(self.nc.sbuf_tensor(name, shape, dt))

    def ps(self, name, shape, dt=F32):
        return self.stack.enter_context(self.nc.psum_tensor(name, shape, dt))

    def sem(self, name):
        return self.stack.enter_context(self.nc.semaphore(name))


def norm_inputs(nc, m, a, s):
    with ExitStack() as stack:
        t = Mem(nc, stack)
        rows = a.vecs.shape[0]
        vrow = t.sb("vrow", [rows, P])
        wa = [t.sb(f"wa{b}", [P, KD, D]) for b in range(2)]
        xc = t.sb("xc", [P, 2, D])
        xt = [s.x1[:, i, :] for i in range(NT)] + [xc[:, i, :] for i in range(2)]
        acc = [t.sb(f"acc{b}", [P, D]) for b in range(4)]
        junk = t.sb("junk", [P, D])
        ss = t.sb("ss", [P, 10])
        root = t.sb("root", [P, 10])
        rstd = t.sb("rstd", [P, 10])
        tmp = t.sb("tmp", [P, 10])
        part = t.sb("part", [P, 2, KD])
        cols = t.sb("cols", [P, 4, KD])
        one = t.sb("one", [P, 1])
        epsb = t.sb("epsb", [P, 1])
        p_v = t.ps("p_v", [P, 512])
        p_c = t.ps("p_c", [P, 512])
        p_t = [t.ps(f"p_t{b}", [P, 512]) for b in range(4)]

        vecs_in, x_in, w_in = t.sem("vecs_in"), [t.sem(f"x_in{g}") for g in range(3)], [t.sem(f"wa_in{b}") for b in range(2)]
        vecs_t, vecs_ok, silu_ok = t.sem("vecs_t"), t.sem("vecs_ok"), t.sem("silu_ok")
        accs, sums, mods = t.sem("accs"), t.sem("sums"), t.sem("mods")
        squares, roots, normed = t.sem("squares"), t.sem("roots"), t.sem("normed")
        turned, moved_a, moved_v, consts_ok = t.sem("turned"), t.sem("moved_a"), t.sem("moved_v"), t.sem("consts_ok")
        dchain = t.sem("dchain")
        groups = [(0, 4), (4, 4), (8, 2)]

        with nc.Block() as block:

            @block.sync
            def _(sp):
                sp.dma_start(vrow[:], a.vecs).then_inc(vecs_in, 16)
                sp.dma_start(s.ident[:], a.ident).then_inc(vecs_in, 16)
                for j in range(2):
                    sp.dma_start(wa[j][:], a.w_ada[:, j * D:(j + 1) * D].rearrange("(k p) n -> p k n", p=P)).then_inc(w_in[j], 16)
                    src = a.x_nat[j * 512:(j + 1) * 512, :]
                    sp.dma_start(s.x1[:, 4 * j:4 * j + 4, :], src.rearrange("(t p) n -> p t n", p=P)).then_inc(x_in[j], 16)
                sp.dma_start(xc[:], a.ctx.rearrange("(t p) n -> p t n", p=P)).then_inc(x_in[2], 16)

            @block.gpsimd
            def _(pool):
                pool.memset(s.ones[:], 1.0).then_inc(consts_ok, 1)
                pool.memset(one[:], 1.0).then_inc(consts_ok, 1)
                pool.memset(epsb[:], EPS).then_inc(consts_ok, 1)

            @block.scalar
            def _(act):
                act.wait_ge(vecs_ok, 1)
                act.activation(s.cond[:], s.vcol[:, 48:64], ACT.Silu).then_inc(silu_ok, 1)
                for g, (t0, n) in enumerate(groups):
                    act.wait_ge(x_in[g], 16)
                    for i in range(t0, t0 + n):
                        act.wait_ge(squares, i)
                        act.activation(junk[:], xt[i], ACT.Square, accum_out=ss[:, i:i + 1]).then_inc(squares, 1)
                act.wait_ge(squares, 10)
                act.wait_ge(consts_ok, 3)
                act.activation(root[:], ss[:], ACT.Sqrt, scale=1.0 / D, bias=epsb[:, 0:1]).then_inc(roots, 1)
                act.wait_ge(mods, 4)
                u = 0
                for g, (t0, n) in enumerate(groups):
                    sh, sc = (0, 1) if g < 2 else (2, 3)
                    for k in range(KD):
                        if u % 2 == 0:
                            act.wait_ge(turned, u + 1)
                            act.activation(s.ht[:, k, t0 * P:(t0 + n) * P], p_t[u % 4][:, 0:n * P], ACT.Identity,
                                           scale=cols[:, sc, k:k + 1], bias=cols[:, sh, k:k + 1]).then_inc(moved_a, 1)
                        u += 1

            @block.vector
            def _(dve):
                c = Counter(dve, dchain)
                dve.wait_ge(vecs_t, 1)
                dve.tensor_copy(s.vcol[:], p_v[:, 0:rows]).then_inc(vecs_ok, 1)
                dve.wait_ge(silu_ok, 1)
                n = 0
                for j in range(2):
                    dve.wait_ge(w_in[j], 16)
                    for k in range(KD):
                        for w in range(2):
                            dst = acc[2 * w + j]
                            cc = s.cond[:, 8 * w + k:8 * w + k + 1]
                            if k == 0:
                                dve.tensor_scalar(dst[:], wa[j][:, k, :], cc, None, ALU.mult).then_inc(accs, 1)
                            else:
                                dve.wait_ge(accs, n - 1)
                                dve.scalar_tensor_tensor(dst[:], wa[j][:, k, :], cc, dst[:], ALU.mult, ALU.add).then_inc(accs, 1)
                            n += 1
                dve.wait_ge(roots, 1)
                c.step(dve.reciprocal(rstd[:], root[:]))
                newton(dve, c, rstd, ss, tmp, D)
                for g, (t0, n_) in enumerate(groups):
                    for i in range(t0, t0 + n_):
                        dve.tensor_scalar(xt[i], xt[i], rstd[:, i:i + 1], None, ALU.mult).then_inc(normed, 1)
                dve.wait_ge(sums, 1)
                for w in range(2):
                    dve.tensor_tensor(cols[:, 2 * w, :], p_c[:, 16 * w:16 * w + 8], s.vcol[:, 0:8], ALU.add).then_inc(mods, 1)
                    c.step(dve.tensor_tensor(part[:, w, :], p_c[:, 16 * w + 8:16 * w + 16], s.vcol[:, 8:16], ALU.add))
                    dve.scalar_tensor_tensor(cols[:, 2 * w + 1, :], part[:, w, :], 1.0, s.vcol[:, 64:72], ALU.add, ALU.mult).then_inc(mods, 1)
                dve.wait_ge(mods, 4)
                u = 0
                for g, (t0, n_) in enumerate(groups):
                    sh, sc = (0, 1) if g < 2 else (2, 3)
                    for k in range(KD):
                        if u % 2 == 1:
                            dve.wait_ge(turned, u + 1)
                            dve.tensor_scalar(s.ht[:, k, t0 * P:(t0 + n_) * P], p_t[u % 4][:, 0:n_ * P],
                                              cols[:, sc, k:k + 1], cols[:, sh, k:k + 1], ALU.mult, ALU.add).then_inc(moved_v, 1)
                        u += 1

            @block.tensor
            def _(pe):
                pe.wait_ge(vecs_in, 32)
                pe.transpose(p_v[:, 0:rows], vrow[:], s.ident[0:rows, 0:rows]).then_inc(vecs_t, 1)
                pe.wait_ge(accs, 32)
                pe.wait_ge(consts_ok, 3)
                for b in range(4):
                    for k in range(KD):
                        last = pe.matmul(p_c[:, 8 * b + k:8 * b + k + 1], acc[b][:, k * P:(k + 1) * P], one[:], start=True, stop=True)
                last.then_inc(sums, 1)
                u = 0
                for g, (t0, n) in enumerate(groups):
                    pe.wait_ge(normed, t0 + n)
                    for k in range(KD):
                        if u >= 4:
                            pe.wait_ge(moved_a if u % 2 == 0 else moved_v, (u - 4) // 2 + 1)
                        for i in range(n):
                            last = pe.transpose(p_t[u % 4][:, i * P:(i + 1) * P], xt[t0 + i][:, k * P:(k + 1) * P], s.ident[:])
                        last.then_inc(turned, 1)
                        u += 1


def newton(dve, c, r, ss, tmp, width, n=None):
    rr, tt, sq = (r[:], tmp[:], ss[:]) if n is None else (r, tmp, ss)
    c.step(dve.tensor_tensor(tt, rr, rr, ALU.mult))
    c.step(dve.tensor_scalar(sq, sq, 1.0 / width, EPS, ALU.mult, ALU.add))
    c.step(dve.tensor_tensor(tt, tt, sq, ALU.mult))
    c.step(dve.tensor_scalar(tt, tt, -0.5, 1.5, ALU.mult, ALU.add))
    c.step(dve.tensor_tensor(rr, rr, tt, ALU.mult))


def project_values(nc, m, a, s):
    with ExitStack() as stack:
        t = Mem(nc, stack)
        wv = t.sb("wv", [P, KD, DN])
        wf = t.sb("wf", [P, KD, DF])
        vrow = [t.sb(f"v_row{b}", [P, DN]) for b in range(2)]
        fmix = t.sb("fmix", [P, 2, DF])
        chan = t.sb("chan", [P, 2, P])
        ab = t.sb("ab", [P, 2, 2 * DF])
        gg = s.x1[:, 0:4, :].rearrange("p a (b n) -> p (a b) n", b=2)
        ft = s.x1[:, 4:6, :]
        dft = [t.sb(f"dft{b}", [P, NT, 2, P]) for b in range(2)]
        wa = [t.sb(f"wa2{b}", [P, 2, D]) for b in range(2)]
        acc = [t.sb(f"acc2{b}", [P, D]) for b in range(2)]
        brow = t.sb("brow", [1, 2, D])
        onerow = t.sb("onerow", [1, P])
        tmp = t.sb("tmp2", [P, KD])
        p_v = [t.ps(f"p_v{b}", [P, 2, 512]) for b in range(2)]
        p_f = [t.ps(f"p_f{b}", [P, 512]) for b in range(2)]
        p_m = t.ps("p_m", [P, 2, 512])

        wv_in, wf_in, fm_in, br_in = t.sem("wv_in"), t.sem("wf_in"), t.sem("fm_in"), t.sem("br_in")
        wa_in = [t.sem(f"wa2_in{b}") for b in range(2)]
        dft_in = [t.sem(f"dft_in{b}") for b in range(2)]
        v_out = [t.sem(f"v_out{b}") for b in range(2)]
        values, values_moved = t.sem("values"), t.sem("values_moved")
        four, four_moved, ones_ok = t.sem("four"), t.sem("four_moved"), t.sem("ones_ok2")
        accs, modsum, modmoved, chain = t.sem("accs2"), t.sem("modsum"), t.sem("modmoved"), t.sem("chain2")

        with nc.Block() as block:

            @block.sync
            def _(sp):
                sp.dma_start(wv[:], a.w_in[:, DF + 2 * DN:].rearrange("(k p) n -> p k n", p=P)).then_inc(wv_in, 16)
                sp.dma_start(wf[:], a.w_in[:, 0:DF].rearrange("(k p) n -> p k n", p=P)).then_inc(wf_in, 16)
                sp.dma_start(fmix[:], a.w_fmix.rearrange("(k p) n -> p k n", p=P)).then_inc(fm_in, 16)
                sp.dma_start(chan[:], a.chan.rearrange("c p n -> p c n")).then_inc(fm_in, 16)
                sp.dma_start(brow[:, 0, :], a.b_ada[:, 2 * D:3 * D]).then_inc(br_in, 16)
                sp.dma_start(brow[:, 1, :], a.b_ada[:, 5 * D:6 * D]).then_inc(br_in, 16)
                for b in range(2):
                    sp.dma_start(dft[b][:], a.dft[b].rearrange("(n p) c m -> p n c m", p=P)).then_inc(dft_in[b], 16)
                for u in range(16):
                    j, k = 2 + u // 4, 2 * (u % 4)
                    if u >= 2:
                        sp.wait_ge(accs, 2 * (u - 1))
                    src = a.w_ada[k * P:(k + 2) * P, j * D:(j + 1) * D]
                    sp.dma_start(wa[u % 2][:], src.rearrange("(k p) n -> p k n", p=P)).then_inc(wa_in[u % 2], 16)
                for i in range(2, NT):
                    sp.wait_ge(four, 14 + i - 1)
                    sp.dma_start(dft[i % 2][:], a.dft[i].rearrange("(n p) c m -> p n c m", p=P)).then_inc(dft_in[i % 2], 16)

            @block.gpsimd
            def _(pool):
                pool.memset(onerow[:], 1.0).then_inc(ones_ok, 1)

            @block.scalar
            def _(act):
                def fourier(u):
                    act.wait_ge(four, u + 1)
                    src = p_f[u % 2]
                    if u < 2:
                        act.activation(ab[:, u, :], src[:], ACT.Copy).then_inc(four_moved, 1)
                    elif u < 6:
                        c_, h = (u - 2) // 2, (u - 2) % 2
                        act.activation(ft[:, c_, h * 512:(h + 1) * 512], src[:], ACT.Copy).then_inc(four_moved, 1)
                    elif u < 14:
                        act.activation(gg[:, u - 6, :], src[:], ACT.Copy).then_inc(four_moved, 1)
                    else:
                        act.activation(s.fout[:, u - 14, :], src[:, 0:DF], ACT.Copy).then_inc(four_moved, 1)

                for i in range(NT + 2):
                    act.wait_ge(values, i + 1)
                    if i >= 2 and i < NT:
                        act.wait_ge(v_out[i % 2], 16 * (i // 2))
                    dst = vrow[i % 2][:] if i < NT else s.vctx[:, i - NT, :]
                    act.activation(dst.rearrange("p (c n) -> p c n", c=2), p_v[i % 2][:, :, 0:DN // 2], ACT.Copy).then_inc(values_moved, 1)
                    if i < NT:
                        act.wait_ge(values_moved, i + 1)
                        act.dma_start(a.v_rows[i * P:(i + 1) * P, :], vrow[i % 2][:]).then_inc(v_out[i % 2], 16)
                for u in range(22):
                    fourier(u)
                for b in range(2):
                    act.wait_ge(v_out[b], 16 * (NT // 2))

            @block.vector
            def _(dve):
                c = Counter(dve, chain)
                n = 0

                def modulation(u):
                    nonlocal n
                    j = u // 4
                    dve.wait_ge(wa_in[u % 2], 16 * (u // 2 + 1))
                    for k in (2 * (u % 4), 2 * (u % 4) + 1):
                        dst, cc = acc[j % 2], s.cond[:, k:k + 1]
                        if k == 0:
                            if j >= 2:
                                dve.wait_ge(modsum, j - 1)
                            dve.tensor_scalar(dst[:], wa[u % 2][:, k % 2, :], cc, None, ALU.mult).then_inc(accs, 1)
                        else:
                            dve.wait_ge(accs, n)
                            dve.scalar_tensor_tensor(dst[:], wa[u % 2][:, k % 2, :], cc, dst[:], ALU.mult, ALU.add).then_inc(accs, 1)
                        n += 1

                def modulation_out(j):
                    dve.wait_ge(modsum, j + 1)
                    if j == 0:
                        dve.tensor_copy(s.gate1[:].rearrange("p (c n) -> p c n", c=2), p_m[:]).then_inc(modmoved, 1)
                    if j == 3:
                        dve.tensor_copy(s.gate2[:].rearrange("p (c n) -> p c n", c=2), p_m[:]).then_inc(modmoved, 1)
                    if j == 1:
                        dve.tensor_tensor(s.shift2[:], p_m[:, 0, 0:KD], s.vcol[:, 24:32], ALU.add).then_inc(modmoved, 1)
                    if j == 2:
                        c.step(dve.tensor_tensor(tmp[:], p_m[:, 0, 0:KD], s.vcol[:, 32:40], ALU.add))
                        dve.scalar_tensor_tensor(s.scale2[:], tmp[:], 1.0, s.vcol[:, 72:80], ALU.add, ALU.mult).then_inc(modmoved, 1)

                for u in range(16):
                    modulation(u)
                    if u % 4 == 3 and u >= 7:
                        modulation_out(u // 4 - 1)
                modulation_out(3)

            @block.tensor
            def _(pe):
                def value_tile(i):
                    if i >= 2:
                        pe.wait_ge(values_moved, i - 1)
                    for h in range(2):
                        for k in range(KD):
                            last = pe.matmul(p_v[i % 2][:, h, 0:DN // 2], s.ht[:, k, i * P:(i + 1) * P],
                                             wv[:, k, h * 384:(h + 1) * 384], start=(k == 0), stop=(k == KD - 1))
                    last.then_inc(values, 1)

                def modulation_sum(j):
                    pe.wait_ge(accs, 8 * (j + 1))
                    if j >= 1:
                        pe.wait_ge(modmoved, j)
                    src = acc[j % 2]
                    if j in (0, 3):
                        for h in range(2):
                            pe.matmul(p_m[:, h, :], s.ones[:], src[:, h * 512:(h + 1) * 512], start=True, stop=False)
                            last = pe.matmul(p_m[:, h, :], onerow[:], brow[:, j // 3, h * 512:(h + 1) * 512], start=False, stop=True)
                    else:
                        for k in range(KD):
                            last = pe.matmul(p_m[:, 0, k:k + 1], src[:, k * P:(k + 1) * P], s.ones[:, 0:1], start=True, stop=True)
                    last.then_inc(modsum, 1)

                def fourier(u):
                    if u >= 2:
                        pe.wait_ge(four_moved, u - 1)
                    dst = p_f[u % 2]
                    if u < 2:
                        for c in range(2):
                            last = pe.matmul(dst[:, c * DF:(c + 1) * DF], chan[:, c, :], fmix[:, u, :], start=True, stop=True)
                    elif u < 6:
                        c, h = (u - 2) // 2, (u - 2) % 2
                        for k in range(KD):
                            last = pe.matmul(dst[:], wf[:, k, c * P:(c + 1) * P], s.ht[:, k, h * 512:(h + 1) * 512],
                                             start=(k == 0), stop=(k == KD - 1))
                    elif u < 14:
                        i = u - 6
                        pe.wait_ge(four_moved, 6)
                        for c in range(2):
                            last = pe.matmul(dst[:], ft[:, c, i * P:(i + 1) * P], ab[:, c, :], start=(c == 0), stop=(c == 1))
                    else:
                        i = u - 14
                        pe.wait_ge(four_moved, 14)
                        pe.wait_ge(dft_in[i % 2], 16 * (i // 2 + 1))
                        for n in range(NT):
                            for c in range(2):
                                last = pe.matmul(dst[:, 0:DF], dft[i % 2][:, n, c, :], gg[:, n, c * DF:(c + 1) * DF],
                                                 start=(n + c == 0), stop=(n == NT - 1 and c == 1))
                    last.then_inc(four, 1)

                pe.wait_ge(wv_in, 16)
                for i in range(NT + 2):
                    value_tile(i)
                pe.wait_ge(fm_in, 32)
                pe.wait_ge(wf_in, 16)
                pe.wait_ge(br_in, 32)
                pe.wait_ge(ones_ok, 1)
                fourier(0)
                fourier(1)
                modulation_sum(0)
                for u in range(2, 6):
                    if u == 4:
                        modulation_sum(1)
                    fourier(u)
                modulation_sum(2)
                modulation_sum(3)
                for u in range(6, 22):
                    fourier(u)


def attention(nc, m, a, s):
    PAIR = 2 * NT
    with ExitStack() as stack:
        t = Mem(nc, stack)
        rope = s.x1[:, 0:2, :]
        rot = t.sb("rot", [P, P])
        mask = t.sb("mask", [P, NT, LOC], BF16)
        eye16 = t.sb("eye16", [P, P], BF16)
        wqk = t.sb("wqk", [P, KD, 2, P])
        vh = t.sb("vh", [P, 16, P])
        table = [t.sb(f"table{h}", [P, 6, LOC]) for h in range(2)]
        plain = [t.sb(f"plain{g}", [P, 512]) for g in range(4)]
        turned = [t.sb(f"turned{g}", [P, 512]) for g in range(2)]
        cpart, spart = t.sb("cpart", [P, 512]), t.sb("spart", [P, 512])
        qwin = [s.x1[:, 2 + h, :] for h in range(2)]
        qctx = [s.x1[:, 4 + h, :] for h in range(2)]
        kwin, kctx = s.x1[:, 6, :], t.sb("kctx", [P, L])
        biased = [t.sb(f"biased{b}", [P, LOC]) for b in range(2)]
        prob = [t.sb(f"prob{b}", [P, KEYS]) for b in range(2)]
        probt = [t.sb(f"probt{b}", [P, KEYS]) for b in range(2)]
        cmax, rmax, nmax = t.sb("cmax", [P, PAIR]), t.sb("rmax", [P, PAIR]), t.sb("nmax", [P, PAIR])
        psum1, psum2, rsum = t.sb("psum1", [P, PAIR]), t.sb("psum2", [P, PAIR]), t.sb("rsum", [P, PAIR])
        p_win = [t.ps(f"p_win{b}", [P, 512]) for b in range(2)]
        p_ctx = [t.ps(f"p_ctx{b}", [P, 512]) for b in range(2)]
        p_t = [t.ps(f"p_tr{b}", [P, 512]) for b in range(2)]
        p_j, p_o = t.ps("p_j", [P, 512]), t.ps("p_o", [P, 512])

        const_in, zeroed = t.sem("const_in"), t.sem("zeroed")
        w_in, v_in, tab_in = t.sem("w_in3"), t.sem("v_in"), [t.sem(f"tab_in{h}") for h in range(2)]
        projected, proj_moved, rotated, roped, padded = (t.sem(n) for n in ("projected", "proj_moved", "rotated", "roped", "padded"))
        scored, maxed, exped, probs_t, pt_win, pt_ctx, weighted, normed = (
            t.sem(n) for n in ("scored", "maxed", "exped", "probs_t", "pt_win", "pt_ctx", "weighted", "normed3"))
        biased_ok = [t.sem(f"biased_ok{h}") for h in range(2)]
        passed = [t.sem("passed_pool"), t.sem("passed_sp")]
        chain, cmaxed = t.sem("chain3"), t.sem("cmaxed")

        with nc.Block() as block:

            @block.sync
            def _(sp):
                for dst, src in ((rope, a.rope.rearrange("c p n -> p c n")), (rot[:], a.rot), (mask[:], a.mask.bitcast(BF16)), (eye16[:], a.eye16.bitcast(BF16))):
                    sp.dma_start(dst, src).then_inc(const_in, 16)
                with sp.Fori(0, HP) as hp:
                    sp.wait_ge(projected, START + hp * 5)
                    for w in range(2):
                        src = a.w_in[:, bass.ds(DF + w * DN + hp * P, P)]
                        sp.dma_start(wqk[:, :, w, :], src.rearrange("(k p) n -> p k n", p=P)).then_inc(w_in, 16)
                    for h in range(2):
                        sp.wait_ge(biased_ok[h], START + hp * NT)
                        for half in range(2):
                            for kind in range(3):
                                first = LEAD - 128 * half - 8 * kind
                                src = bass.AP(a.rpb.tensor, (hp * 2 + h) * RPB + first, [[PITCH, QR], [1, QC], [1, LOC]])
                                sp.dma_start(table[h][:, 3 * half + kind, :], src).then_inc(tab_in[h], 16)
                        if h == 0:
                            sp.wait_ge(weighted, START + hp * PAIR)
                            sp.sem_inc(passed[1], 1)
                            for j in range(4):
                                for g in range(4):
                                    src = a.v_rows[g * 4 * GW:(g + 1) * 4 * GW, bass.ds(hp * P, P)]
                                    src = src.rearrange("(r c) n -> r c n", c=GW)[:, COL0[j]:COL0[j] + KC, :]
                                    sp.dma_start(vh[:, 4 * j + g, :], src).then_inc(v_in, 16)

            @block.gpsimd
            def _(pool):
                for sem in (projected, weighted, scored, proj_moved, roped, padded, probs_t, exped, pt_win, pt_ctx, normed, *biased_ok):
                    pool.sem_inc(sem, START)
                for h in range(2):
                    pool.memset(qwin[h], 0.0).then_inc(zeroed, 1)
                    pool.memset(qctx[h], 0.0).then_inc(zeroed, 1)
                pool.wait_ge(zeroed, 4)
                with pool.Fori(0, HP) as hp:
                    pool.wait_ge(scored, START + hp * PAIR)
                    for g in range(2):
                        pool.wait_ge(proj_moved, START + hp * 5 + g + 1)
                        pool.sem_inc(passed[0], 1)
                        for src, dst in ((plain[g], qctx), (turned[g], qwin)):
                            if src is turned[g]:
                                pool.wait_ge(roped, START + hp * 4 + g + 1)
                                pool.sem_inc(passed[0], 1)
                            for h in range(2):
                                rows = slice(HD * h, HD * h + HD)
                                grid = src[rows, :].rearrange("p (r j c) -> p j r c", r=QR, j=4)[:, :, ::-1, ::-1]
                                tile = dst[h][rows, g * 512:(g + 1) * 512].rearrange("p (j r c) -> p j r c", r=QR, j=4)
                                pool.tensor_copy(tile, grid).then_inc(padded, 1)

            @block.scalar
            def _(act):
                with act.Fori(0, HP) as hp:
                    for g in range(5):
                        act.wait_ge(projected, START + hp * 5 + g + 1)
                        if g == 0:
                            act.wait_ge(roped, START + hp * 4)
                            act.wait_ge(padded, START + hp * 8)
                            act.wait_ge(scored, START + hp * PAIR)
                        src = (p_j, p_o)[g % 2]
                        if g < 4:
                            act.activation(plain[g][:], src[:], ACT.Copy, scale=HD ** -0.5 if g < 2 else 1.0).then_inc(proj_moved, 1)
                        else:
                            act.activation(kctx[:], src[:, 0:L], ACT.Copy).then_inc(proj_moved, 1)
                    for n in range(PAIR + 1):
                        b = n % 2
                        if n < PAIR:
                            act.wait_ge(maxed, hp * PAIR + n + 1)
                            act.wait_ge(probs_t, START + hp * PAIR + max(n - 1, 0))
                            act.activation(prob[b][:, 0:LOC], biased[b][:], ACT.Exp, bias=nmax[:, n:n + 1],
                                           accum_out=psum1[:, n:n + 1])
                            act.activation(prob[b][:, LOC:KEYS], p_ctx[b][:, 0:L], ACT.Exp, bias=nmax[:, n:n + 1],
                                           accum_out=psum2[:, n:n + 1]).then_inc(exped, 1)
                        if n >= 1:
                            act.wait_ge(probs_t, START + hp * PAIR + n)
                            act.wait_ge(weighted, START + hp * PAIR + max(n - 2, 0))
                            act.activation(probt[1 - b][:, 0:LOC], p_t[0][:, 0:LOC], ACT.Copy).then_inc(pt_win, 1)

            @block.vector
            def _(dve):
                dve.wait_ge(const_in, 64)
                with dve.Fori(0, HP) as hp:
                    c = Counter(dve, chain, hp * 12)
                    for g in range(4):
                        half = slice((g % 2) * 512, (g % 2 + 1) * 512)
                        dve.wait_ge(proj_moved, START + hp * 5 + g + 1)
                        dve.wait_ge(roped, START + hp * 4 + g)
                        c.step(dve.tensor_tensor(cpart[:], plain[g][:], rope[:, 0, half], ALU.mult))
                        dve.wait_ge(rotated, hp * 4 + g + 1)
                        c.step(dve.tensor_tensor(spart[:], p_t[g % 2][:], rope[:, 1, half], ALU.mult))
                        if g == 0:
                            dve.wait_ge(padded, START + hp * 8)
                        if g == 2:
                            dve.wait_ge(scored, START + hp * PAIR)
                        dst = turned[g][:] if g < 2 else kwin[:, half]
                        dve.tensor_tensor(dst, cpart[:], spart[:], ALU.add).then_inc(roped, 1)
                    for n in range(PAIR + 2):
                        h, i, b = n // NT, n % NT, n % 2
                        if n < PAIR:
                            dve.wait_ge(scored, START + hp * PAIR + n + 1)
                            if i == 0:
                                dve.wait_ge(tab_in[h], (hp + 1) * 96)
                            dve.wait_ge(exped, START + hp * PAIR + max(n - 1, 0))
                            dve.tensor_reduce(cmax[:, n:n + 1], p_ctx[b][:, 0:L], AX.X, ALU.max).then_inc(cmaxed, 1)
                            kind = 3 * (i // 4) + KIND[i % 4]
                            dve.tensor_tensor_reduce(biased[b][:], p_win[b][:, 0:LOC], table[h][:, kind, :], 1.0, LOWEST,
                                                     ALU.add, ALU.max, rmax[:, n:n + 1]).then_inc(biased_ok[h], 1)
                            dve.wait_ge(cmaxed, hp * PAIR + n + 1)
                            dve.wait_ge(biased_ok[h], START + hp * NT + i + 1)
                            dve.tensor_scalar(nmax[:, n:n + 1], rmax[:, n:n + 1], cmax[:, n:n + 1], -1.0, ALU.max, ALU.mult).then_inc(maxed, 1)
                        if 1 <= n <= PAIR:
                            dve.wait_ge(probs_t, START + hp * PAIR + n)
                            dve.wait_ge(weighted, START + hp * PAIR + max(n - 2, 0))
                            dve.tensor_copy(probt[1 - b][:, LOC:KEYS], p_t[1][:, 0:L]).then_inc(pt_ctx, 1)
                        if n in (NT + 1, PAIR + 1):
                            h = n // NT - 1
                            cols = slice(NT * h, NT * h + NT)
                            dve.wait_ge(exped, START + hp * PAIR + NT * (h + 1))
                            c.step(dve.tensor_tensor(rsum[:, cols], psum1[:, cols], psum2[:, cols], ALU.add))
                            c.step(dve.reciprocal(rsum[:, cols], rsum[:, cols]))
                            dve.wait_ge(weighted, START + hp * PAIR + NT * (h + 1))
                            dst = s.na[:, :, bass.ds((hp * 2 + h) * HD, HD)]
                            dve.tensor_tensor(dst, p_o[:].rearrange("p (i d) -> p i d", i=NT),
                                              rsum[:, cols].unsqueeze(2).to_broadcast([P, NT, HD]), ALU.mult).then_inc(normed, 1)
                    assert c.n == 12, c.n

            @block.tensor
            def _(pe):
                pe.wait_ge(const_in, 64)
                pe.wait_ge(zeroed, 4)
                with pe.Fori(0, HP) as hp:
                    def project(g):
                        dst = (p_j, p_o)[g % 2]
                        if g == 0:
                            pe.wait_ge(w_in, (hp + 1) * 32)
                            pe.wait_ge(proj_moved, START + hp * 5)
                        elif g == 1:
                            pe.wait_ge(normed, START + hp * 2)
                        else:
                            pe.wait_ge(proj_moved, START + hp * 5 + g - 1)
                        cols = slice((g % 2) * 512, (g % 2 + 1) * 512) if g < 4 else slice(N, N + L)
                        for k in range(KD):
                            last = pe.matmul(dst[:, 0:cols.stop - cols.start], wqk[:, k, 0 if g < 2 else 1, :], s.ht[:, k, cols],
                                             start=(k == 0), stop=(k == KD - 1))
                        last.then_inc(projected, 1)

                    def rotate(g):
                        pe.wait_ge(proj_moved, START + hp * 5 + g + 1)
                        if g == 0:
                            pe.wait_ge(pt_win, START + hp * PAIR)
                        elif g == 1:
                            pe.wait_ge(pt_ctx, START + hp * PAIR)
                        else:
                            pe.wait_ge(roped, START + hp * 4 + g - 1)
                        pe.matmul(p_t[g % 2][:], rot[:], plain[g][:], start=True, stop=True).then_inc(rotated, 1)

                    def score(n):
                        h, i, b = n // NT, n % NT, n % 2
                        pe.wait_ge(exped, START + hp * PAIR + max(n - 1, 0))
                        q = slice(i * P, (i + 1) * P)
                        keys = kwin.rearrange("p (r c) -> p r c", c=GW)[:, 4 * (i // 4):4 * (i // 4) + KR, COL0[i % 4]:COL0[i % 4] + KC]
                        pe.matmul(p_win[b][:, 0:LOC], qwin[h][:, q], keys, start=True, stop=False)
                        pe.matmul(p_win[b][:, 0:LOC], eye16[:], mask[:, i, :], start=False, stop=True)
                        pe.matmul(p_ctx[b][:, 0:L], qctx[h][:, q], kctx[:], start=True, stop=True).then_inc(scored, 1)

                    def turn(n):
                        b = n % 2
                        pe.wait_ge(exped, START + hp * PAIR + n + 1)
                        pe.wait_ge(pt_win, START + hp * PAIR + n)
                        pe.wait_ge(pt_ctx, START + hp * PAIR + n)
                        for k in range(KEYS // P):
                            dst = p_t[0][:, k * P:(k + 1) * P] if k < 3 else p_t[1][:, (k - 3) * P:(k - 2) * P]
                            last = pe.transpose(dst, prob[b][:, k * P:(k + 1) * P], s.ident[:])
                        last.then_inc(probs_t, 1)

                    def weigh(n):
                        h, i, b = n // NT, n % NT, n % 2
                        pe.wait_ge(pt_win, START + hp * PAIR + n + 1)
                        pe.wait_ge(pt_ctx, START + hp * PAIR + n + 1)
                        if n == 0:
                            pe.wait_ge(v_in, (hp + 1) * 256)
                        if i == 0:
                            pe.wait_ge(normed, START + hp * 2 + h)
                        for k in range(KEYS // P):
                            if k < 3:
                                v = vh[:, 4 * (i % 4) + i // 4 + k, h * HD:(h + 1) * HD]
                            else:
                                v = vc[k - 3][:, h * HD:(h + 1) * HD]
                            last = pe.matmul(p_o[:, i * HD:(i + 1) * HD], probt[b][:, k * P:(k + 1) * P], v,
                                             start=(k == 0), stop=(k == KEYS // P - 1))
                        last.then_inc(weighted, 1)

                    vc = [s.vctx[:, k, bass.ds(hp * P, P)] for k in range(2)]
                    project(0)
                    project(1)
                    rotate(0)
                    project(2)
                    rotate(1)
                    project(3)
                    rotate(2)
                    project(4)
                    rotate(3)
                    pe.wait_ge(padded, START + (hp + 1) * 8)
                    pe.wait_ge(roped, START + (hp + 1) * 4)
                    pe.wait_ge(proj_moved, START + (hp + 1) * 5)
                    for n in range(PAIR + 2):
                        if n < PAIR:
                            score(n)
                        if 1 <= n <= PAIR:
                            turn(n - 1)
                        if n >= 2:
                            weigh(n - 2)


def mix_and_route(nc, m, a, s):
    with ExitStack() as stack:
        t = Mem(nc, stack)
        wo = t.sb("wo", [P, KD, D])
        free = s.ht[:].rearrange("p k n -> p (k n)")
        yrow = free[:, 0:4 * D].rearrange("p (i n) -> p i n", i=4)
        yt = free[:, 4 * D:8 * D].rearrange("p (k n) -> p k n", k=KD)
        xp = free[:, 8 * D:10 * D].rearrange("p (b n) -> p b n", b=2)
        wr = t.sb("wr", [P, KD, NG + NE])
        before = t.sb("before", [P, P])
        desc, base, blk, ids = t.sb("desc", [P, NT, EPG]), t.sb("base", [P, NE]), t.sb("blk", [1, OVB, NE]), t.sb("ids", [P, 2, NT, 4], I32)
        junk = t.sb("junk4", [P, D])
        epsb = t.sb("epsb4", [P, 1])
        ss = t.sb("ss4", [P, 3, NT])
        root, rstd, tmp = t.sb("root4", [P, 3, NT]), t.sb("rstd4", [P, 3, NT]), t.sb("tmp4", [P, 3, NT])
        empty = t.sb("empty", [P, SLOTS * 4 // P], I32)
        lg = t.sb("lg", [P, NT, NG + NE])
        p_y = [t.ps(f"p_y{b}", [P, 2, 512]) for b in range(2)]
        p_t = [t.ps(f"p_t4{b}", [P, 512]) for b in range(2)]
        p_l, p_r = t.ps("p_l", [P, 512]), t.ps("p_r", [P, 2, NE * NT])

        w_in, c_in, xp_in = t.sem("wo_in"), t.sem("c4_in"), [t.sem(f"xp_in{b}") for b in range(2)]
        pool_ok, squared, rooted, scaled = t.sem("pool_ok4"), t.sem("squared4"), t.sem("rooted4"), t.sem("scaled4")
        turned, t_act, t_dve = t.sem("turned4"), t.sem("t_act4"), t.sem("t_dve4")
        mixed, added, squared2, rooted2, scaled2 = t.sem("mixed"), t.sem("added"), t.sem("squared5"), t.sem("rooted5"), t.sem("scaled5")
        logits, logits_moved, h_out = t.sem("logits"), t.sem("logits_moved"), t.sem("h_out")
        chosen, ranked, slots_ok, exps_in, exps = t.sem("chosen"), t.sem("ranked"), t.sem("slots_ok"), t.sem("exps_in"), t.sem("exps")
        table_empty, scattered, chain = t.sem("table_empty"), t.sem("scattered"), t.sem("chain4")
        small = lambda name, *shape: t.sb(name, [P, *shape])
        gmax, goh, gsum, gdif = small("gmax", NT), small("goh", NT, NG), small("gsum", NT), small("gdif", NT, NG)
        lsel, lpart, lmax = small("lsel", NT, EPG), small("lpart", NT, NG, EPG), small("lmax", 2, NT)
        eoh, key, kmax = small("eoh", 2, NT, EPG), small("key", NT, EPG), small("kmax", NT)
        wexp, gates, den = small("wexp", NT), small("gates", 2, NT), small("den", NT)
        one_e, both = small("one_e", 2, NT, NE), small("both", NT, NE)
        offs, rank, count = small("offs", NT + 1, NE), small("rank", NT, NE), small("count", NT, NE)
        over, upto, ovb = small("over", NE), small("upto", NE), small("ovb", NE)
        pick, rk, bs, ob = small("pick", NT, NE), small("rk", 2, NT), small("bs", 2, NT), small("ob", 2, NT)
        slot = t.sb("slot", [P, 2, NT], I32)
        cmpb, cntb = t.sb("cmpb", [1, OVB, NE]), t.sb("cntb", [1, OVB + 1])

        with nc.Block() as block:

            @block.sync
            def _(sp):
                for dst, src in ((before, a.before), (desc, a.desc), (base, a.base), (blk, a.blk), (ids, a.ids)):
                    sp.dma_start(dst[:], src).then_inc(c_in, 16)
                sp.dma_start(wr[:], a.w_router.rearrange("(k p) n -> p k n", p=P)).then_inc(c_in, 16)
                sp.dma_start(wo[:], a.w_out.rearrange("(k p) n -> p k n", p=P)).then_inc(w_in, 16)
                for i in range(NT):
                    if i >= 2:
                        sp.wait_ge(added, 2 * (i - 1))
                    sp.dma_start(xp[:, i % 2, :], a.x_perm[i * P:(i + 1) * P, :]).then_inc(xp_in[i % 2], 16)

            @block.gpsimd
            def _(pool):
                pool.memset(epsb[:], EPS).then_inc(pool_ok, 1)
                pool.memset(offs[:, 0, :], 0.0).then_inc(pool_ok, 1)
                pool.memset(over[:], 0.0).then_inc(pool_ok, 1)
                pool.memset(empty[:], SKIP).then_inc(pool_ok, 1)
                pool.wait_ge(pool_ok, 4)
                pool.dma_start(a.slot_rows.rearrange("(p n) c -> p (n c)", p=P), empty[:]).then_inc(table_empty, 16)
                pool.wait_ge(table_empty, 16)
                pool.wait_ge(slots_ok, 3)
                for k in range(2):
                    for i in range(NT):
                        pool.indirect_dma_start(a.slot_rows, bass.IndirectOffsetOnAxis(ap=slot[:, k, i:i + 1], axis=0),
                                                ids[:, k, i, :], None, bounds_check=SLOTS - 1).then_inc(scattered, 16)
                pool.wait_ge(scattered, 16 * 2 * NT)

            def norm_groups(act):
                for i in range(NT):
                    for w, (src, width) in enumerate(((s.fout[:, i, :], DF), (s.na[:, i, :], DN))):
                        act.wait_ge(squared, 2 * i + w)
                        act.activation(junk[:, 0:width], src, ACT.Square, accum_out=ss[:, w, i:i + 1]).then_inc(squared, 1)
                act.wait_ge(squared, 2 * NT)
                act.wait_ge(pool_ok, 4)
                for w, width in enumerate((DF, DN)):
                    act.activation(root[:, w, :], ss[:, w, :], ACT.Sqrt, scale=1.0 / width, bias=epsb[:, 0:1]).then_inc(rooted, 1)

            @block.scalar
            def _(act):
                norm_groups(act)
                for g in range(2):
                    for k in range(0, KD, 2):
                        act.wait_ge(turned, 16 * g + k + 1)
                        if g == 1 and k == 0:
                            act.wait_ge(mixed, 4)
                        act.activation(yt[:, k, :], p_t[k % 2][:], ACT.Copy, scale=s.vcol[:, 80 + k:81 + k]).then_inc(t_act, 1)
                    for i in range(4 * g, 4 * g + 4):
                        act.wait_ge(added, 2 * (i + 1))
                        act.wait_ge(squared2, i)
                        act.activation(junk[:], s.x1[:, i, :], ACT.Square, accum_out=ss[:, 2, i:i + 1]).then_inc(squared2, 1)
                    act.wait_ge(squared2, 4 * g + 4)
                    act.activation(root[:, 2, 4 * g:4 * g + 4], ss[:, 2, 4 * g:4 * g + 4], ACT.Sqrt, scale=1.0 / D,
                                   bias=epsb[:, 0:1]).then_inc(rooted2, 1)
                    for i in range(4):
                        act.wait_ge(scaled2, 4 * g + i + 1)
                        n = 4 * g + i
                        act.dma_start(a.h_rows[n * P:(n + 1) * P, :], yrow[:, i, :]).then_inc(h_out, 16)
                    for k in range(0, KD, 2):
                        act.wait_ge(turned, 16 * g + 8 + k + 1)
                        act.activation(yt[:, k, :], p_t[k % 2][:], ACT.Identity, scale=s.scale2[:, k:k + 1],
                                       bias=s.shift2[:, k:k + 1]).then_inc(t_act, 1)
                act.wait_ge(exps_in, 1)
                act.activation(gdif[:], gdif[:], ACT.Exp).then_inc(exps, 1)
                act.wait_ge(exps_in, 2)
                act.activation(wexp[:], wexp[:], ACT.Exp).then_inc(exps, 1)
                act.wait_ge(h_out, 16 * NT)

            @block.vector
            def _(dve):
                c = Counter(dve, chain)
                step = c.step
                tt, ts, stt = dve.tensor_tensor, dve.tensor_scalar, dve.scalar_tensor_tensor
                dve.wait_ge(rooted, 2)
                step(dve.reciprocal(rstd[:, 0:2, :], root[:, 0:2, :]))
                for w, width in enumerate((DF, DN)):
                    newton(dve, c, rstd[:, w, :], ss[:, w, :], tmp[:, w, :], width, n=NT)
                dve.wait_ge(c_in, 96)
                for g in range(2):
                    for i in range(4):
                        n = 4 * g + i
                        if g == 1:
                            dve.wait_ge(h_out, 64)
                            dve.wait_ge(turned, 16)
                        ts(yrow[:, i, 0:DF], s.fout[:, n, :], rstd[:, 0, n:n + 1], None, ALU.mult).then_inc(scaled, 1)
                        ts(yrow[:, i, DF:D], s.na[:, n, :], rstd[:, 1, n:n + 1], None, ALU.mult).then_inc(scaled, 1)
                    for k in range(1, KD, 2):
                        dve.wait_ge(turned, 16 * g + k + 1)
                        if g == 1 and k == 1:
                            dve.wait_ge(mixed, 4)
                        ts(yt[:, k, :], p_t[k % 2][:], s.vcol[:, 80 + k:81 + k], None, ALU.mult).then_inc(t_dve, 1)
                    for i in range(4):
                        n = 4 * g + i
                        dve.wait_ge(mixed, n + 1)
                        dve.wait_ge(xp_in[n % 2], 16 * (n // 2 + 1))
                        x1 = s.x1[:, n, :]
                        dve.tensor_tensor(x1.rearrange("p (c n) -> p c n", c=2), p_y[n % 2][:],
                                          s.gate1[:].rearrange("p (c n) -> p c n", c=2), ALU.mult).then_inc(added, 1)
                        dve.wait_ge(added, 2 * n + 1)
                        dve.tensor_tensor(x1, x1, xp[:, n % 2, :], ALU.add).then_inc(added, 1)
                    dve.wait_ge(rooted2, g + 1)
                    four = slice(4 * g, 4 * g + 4)
                    step(dve.reciprocal(rstd[:, 2, four], root[:, 2, four]))
                    newton(dve, c, rstd[:, 2, four], ss[:, 2, four], tmp[:, 2, four], D, n=4)
                    for i in range(4):
                        n = 4 * g + i
                        ts(yrow[:, i, :], s.x1[:, n, :], rstd[:, 2, n:n + 1], None, ALU.mult).then_inc(scaled2, 1)
                    for k in range(1, KD, 2):
                        dve.wait_ge(turned, 16 * g + 8 + k + 1)
                        ts(yt[:, k, :], p_t[k % 2][:], s.scale2[:, k:k + 1], s.shift2[:, k:k + 1], ALU.mult, ALU.add).then_inc(t_dve, 1)
                    dve.wait_ge(logits, g + 1)
                    step(dve.tensor_copy(lg[:, four, :], p_l[:, 0:4 * (NG + NE)].rearrange("p (i n) -> p i n", i=4)))
                    dve.sem_inc(logits_moved, 1)

                def bc(x, n):
                    return x.unsqueeze(2).to_broadcast([P, NT, n])

                def first_match(dst, values, top, d):
                    n = values.shape[2]
                    step(tt(key[:, :, 0:n], values, bc(top, n), ALU.is_equal))
                    step(tt(key[:, :, 0:n], key[:, :, 0:n], d, ALU.mult))
                    step(dve.tensor_reduce(kmax[:], key[:, :, 0:n], AX.X, ALU.max))
                    step(tt(dst, key[:, :, 0:n], bc(kmax[:], n), ALU.is_equal))

                lgg, lge = lg[:, :, 0:NG], lg[:, :, NG:NG + NE].rearrange("p i (g e) -> p i g e", g=NG)
                step(dve.tensor_reduce(gmax[:], lgg, AX.X, ALU.max))
                step(tt(gdif[:], lgg, bc(gmax[:], NG), ALU.subtract))
                dve.sem_inc(exps_in, 1)
                first_match(goh[:], lgg, gmax[:], desc[:, :, EPG - NG:EPG])
                step(tt(lpart[:], lge, goh[:].unsqueeze(3).to_broadcast([P, NT, NG, EPG]), ALU.mult))
                step(tt(lsel[:], lpart[:, :, 0, :], lpart[:, :, 1, :], ALU.add))
                step(tt(lsel[:], lsel[:], lpart[:, :, 2, :], ALU.add))
                step(tt(lsel[:], lsel[:], lpart[:, :, 3, :], ALU.add))
                step(dve.tensor_reduce(lmax[:, 0, :], lsel[:], AX.X, ALU.max))
                first_match(eoh[:, 0], lsel[:], lmax[:, 0, :], desc[:])
                step(stt(lsel[:], eoh[:, 0], NEG, lsel[:], ALU.mult, ALU.add))
                step(dve.tensor_reduce(lmax[:, 1, :], lsel[:], AX.X, ALU.max))
                first_match(eoh[:, 1], lsel[:], lmax[:, 1, :], desc[:])
                step(tt(wexp[:], lmax[:, 1, :], lmax[:, 0, :], ALU.subtract))
                dve.sem_inc(exps_in, 1)
                for k in range(2):
                    step(tt(one_e[:, k].rearrange("p i (g e) -> p i g e", g=NG), goh[:].unsqueeze(3).to_broadcast([P, NT, NG, EPG]),
                            eoh[:, k].unsqueeze(2).to_broadcast([P, NT, NG, EPG]), ALU.mult))
                step(tt(both[:], one_e[:, 0], one_e[:, 1], ALU.add))
                dve.sem_inc(chosen, 1)
                dve.wait_ge(exps, 1)
                step(dve.tensor_reduce(gsum[:], gdif[:], AX.X, ALU.add))
                dve.wait_ge(exps, 2)
                step(ts(den[:], wexp[:], 1.0, None, ALU.add))
                step(tt(den[:], den[:], gsum[:], ALU.mult))
                step(dve.reciprocal(gates[:, 0, :], den[:]))
                step(tt(gates[:, 1, :], gates[:, 0, :], wexp[:], ALU.mult))
                for k in range(2):
                    dve.tensor_copy(ids[:, k, :, 2].bitcast(F32), gates[:, k, :]).then_inc(slots_ok, 1)
                dve.wait_ge(ranked, 1)
                step(dve.tensor_copy(count[:], p_r[:, 1, :].rearrange("p (i e) -> p i e", e=NE)))
                for i in range(NT):
                    step(tt(offs[:, i + 1, :], offs[:, i, :], count[:, i, :], ALU.add))
                step(tt(rank[:], p_r[:, 0, :].rearrange("p (i e) -> p i e", e=NE), offs[:, 0:NT, :], ALU.add))
                for i in range(1, N // CAP):
                    step(stt(over[:], offs[:, NT, :], float(CAP * i), over[:], ALU.is_gt, ALU.add))
                step(dve.tensor_tensor_scan(upto[:], s.ones[:, 0:NE], over[:], 0.0, ALU.mult, ALU.add))
                step(tt(ovb[:], upto[:], over[:], ALU.subtract))
                step(ts(ovb[:], ovb[:], float(CAP), float((NE - 1) * CAP), ALU.mult, ALU.add))
                for k in range(2):
                    for dst, src in ((rk, rank[:]), (bs, base[:].unsqueeze(1).to_broadcast([P, NT, NE])), (ob, ovb[:].unsqueeze(1).to_broadcast([P, NT, NE]))):
                        step(tt(pick[:], one_e[:, k], src, ALU.mult))
                        step(dve.tensor_reduce(dst[:, k, :], pick[:], AX.X, ALU.add))
                step(tt(ob[:], ob[:], bs[:], ALU.subtract))
                step(tt(bs[:], bs[:], rk[:], ALU.add))
                step(ts(rk[:], rk[:], float(CAP), None, ALU.is_ge))
                step(tt(rk[:], rk[:], ob[:], ALU.mult))
                step(tt(rk[:], rk[:], bs[:], ALU.add))
                dve.tensor_copy(slot[:], rk[:]).then_inc(slots_ok, 1)
                step(tt(cmpb[:], upto[0:1, :].unsqueeze(1).to_broadcast([1, OVB, NE]), blk[:], ALU.is_le))
                step(dve.tensor_reduce(cntb[:, 0:OVB], cmpb[:], AX.X, ALU.add))
                step(ts(cntb[:, 0:OVB], cntb[:, 0:OVB], float(NE - 1), None, ALU.min))
                step(dve.tensor_copy(cntb[:, OVB:OVB + 1], upto[0:1, NE - 1:NE]))
                step(dve.tensor_copy(s.blocks[:], cntb[:]))

            @block.tensor
            def _(pe):
                def turn(g, second):
                    for k in range(KD):
                        u = 16 * g + 8 * second + k
                        if u >= 2:
                            pe.wait_ge(t_act if k % 2 == 0 else t_dve, (u - 2) // 2 + 1)
                        for i in range(4):
                            last = pe.transpose(p_t[k % 2][:, i * P:(i + 1) * P], yrow[:, i, k * P:(k + 1) * P], s.ident[:])
                        last.then_inc(turned, 1)
                    pe.wait_ge(t_act, 4 * (2 * g + second + 1))
                    pe.wait_ge(t_dve, 4 * (2 * g + second + 1))

                pe.wait_ge(c_in, 96)
                for g in range(2):
                    pe.wait_ge(scaled, 8 * (g + 1))
                    turn(g, 0)
                    pe.wait_ge(w_in, 16)
                    for i in range(4):
                        n = 4 * g + i
                        if n >= 2:
                            pe.wait_ge(added, 2 * (n - 2) + 1)
                        for h in range(2):
                            for k in range(KD):
                                last = pe.matmul(p_y[n % 2][:, h, :], yt[:, k, i * P:(i + 1) * P], wo[:, k, h * 512:(h + 1) * 512],
                                                 start=(k == 0), stop=(k == KD - 1))
                        last.then_inc(mixed, 1)
                    pe.wait_ge(scaled2, 4 * (g + 1))
                    turn(g, 1)
                    if g == 1:
                        pe.wait_ge(logits_moved, 1)
                    for i in range(4):
                        for k in range(KD):
                            last = pe.matmul(p_l[:, i * 36:(i + 1) * 36], yt[:, k, i * P:(i + 1) * P], wr[:, k, :],
                                             start=(k == 0), stop=(k == KD - 1))
                    last.then_inc(logits, 1)
                pe.wait_ge(chosen, 1)
                flat = both[:].rearrange("p i e -> p (i e)")
                pe.matmul(p_r[:, 0, :], before[:], flat, start=True, stop=True)
                pe.matmul(p_r[:, 1, :], s.ones[:], flat, start=True, stop=True).then_inc(ranked, 1)


class ExpertSteps:

    def __init__(self, t, a, s, buf, run):
        self.a, self.s, self.buf = a, s, buf
        self.gu_in = [t.sem(f"{run}_gu_in{b}") for b in range(2)]
        self.d_in = [t.sem(f"{run}_d_in{b}") for b in range(2)]
        self.sid_in = [t.sem(f"{run}_sid_in{b}") for b in range(2)]
        self.gathered = [t.sem(f"{run}_gathered{b}") for b in range(2)]
        self.scattered = [t.sem(f"{run}_scattered{b}") for b in range(2)]
        self.x_turned, self.x_act, self.x_dve = t.sem(f"{run}_x_turned"), t.sem(f"{run}_x_act"), t.sem(f"{run}_x_dve")
        self.gateups, self.silu_ok, self.h_ok = t.sem(f"{run}_gateups"), t.sem(f"{run}_silu_ok"), t.sem(f"{run}_h_ok")
        self.h_turned, self.ht_moved = t.sem(f"{run}_h_turned"), t.sem(f"{run}_ht_moved")
        self.downs, self.y_ok = t.sem(f"{run}_downs"), t.sem(f"{run}_y_ok")
        self.passed, self.sp_passed = t.sem(f"{run}_passed"), t.sem(f"{run}_sp_passed")

    def primed(self):
        return [self.x_turned, self.x_act, self.x_dve, self.gateups, self.h_ok, self.h_turned, self.ht_moved,
                self.downs, self.y_ok]

    def load_gate_up(self, sp, b, e):
        for dst, src in ((self.buf.wg, self.a.w_gate), (self.buf.wu, self.a.w_up)):
            sp.dma_start(dst[b][:], src[e].rearrange("(k p) n -> p k n", p=P)).then_inc(self.gu_in[b], 16)

    def load_down(self, sp, b, e):
        sp.dma_start(self.buf.wd[b][:], self.a.w_down[e].rearrange("(k p) n -> p k n", p=P)).then_inc(self.d_in[b], 16)

    def load_slots(self, sp, b, block):
        sp.dma_start(self.buf.sid[b][:], self.a.slot_blocks[block]).then_inc(self.sid_in[b], 16)

    def gather(self, pool, b, it, turned):
        pool.wait_ge(self.sid_in[b], (it + 1) * 16)
        pool.wait_ge(self.x_turned, START + turned)
        pool.sem_inc(self.passed, 1)
        pool.indirect_dma_start(self.buf.xg[b][:], None, self.a.h_rows, bass.IndirectOffsetOnAxis(ap=self.buf.sid[b][:, 0:1], axis=0),
                                bounds_check=N - 1, oob_is_err=False).then_inc(self.gathered[b], 16)

    def scatter(self, pool, n, b):
        pool.wait_ge(self.y_ok, START + n + 1)
        pool.sem_inc(self.passed, 1)
        pool.indirect_dma_start(self.a.y_rows, bass.IndirectOffsetOnAxis(ap=self.buf.sid[b][:, 1:2], axis=0), self.buf.y[b][:], None,
                                bounds_check=2 * N - 1, oob_is_err=False).then_inc(self.scattered[b], 16)

    def turn_x(self, pe, n, b, it):
        pe.wait_ge(self.gathered[b], (it + 1) * 16)
        pe.wait_ge(self.x_act, START + n)
        pe.wait_ge(self.x_dve, START + n)
        for k in range(KD):
            last = pe.transpose(self.buf.p_x[k // 4][:, k % 4, :], self.buf.xg[b][:, k * P:(k + 1) * P], self.s.ident[:])
        last.then_inc(self.x_turned, 1)

    def move_x(self, eng, n, b, used):
        eng.wait_ge(self.x_turned, START + n + 1)
        eng.wait_ge(self.gateups, START + used)
        on_act = eng is self.s.act
        for k in range(0, 4) if on_act else range(4, 8):
            dst, src = self.buf.xt[b][:, k, :], self.buf.p_x[k // 4][:, k % 4, :]
            sc, sh = self.s.scale2[:, k:k + 1], self.s.shift2[:, k:k + 1]
            if on_act:
                last = eng.activation(dst, src, ACT.Identity, scale=sc, bias=sh)
            else:
                last = eng.tensor_scalar(dst, src, sc, sh, ALU.mult, ALU.add)
        last.then_inc(self.x_act if on_act else self.x_dve, 1)

    def gate_up(self, pe, n, b, it):
        pe.wait_ge(self.gu_in[b], (it + 1) * 32)
        pe.wait_ge(self.x_act, START + n + 1)
        pe.wait_ge(self.x_dve, START + n + 1)
        pe.wait_ge(self.h_ok, START + n)
        for w, dst in ((self.buf.wg[b], self.buf.p_g), (self.buf.wu[b], self.buf.p_u)):
            for k in range(KD):
                last = pe.matmul(dst[:], self.buf.xt[b][:, k, :], w[:, k, :], start=(k == 0), stop=(k == KD - 1))
        last.then_inc(self.gateups, 1)

    def silu(self, act, n):
        act.wait_ge(self.gateups, START + n + 1)
        act.wait_ge(self.h_ok, START + n)
        act.activation(self.buf.silu[:], self.buf.p_g[:], ACT.Silu).then_inc(self.silu_ok, 1)

    def multiply(self, dve, n):
        dve.wait_ge(self.silu_ok, n + 1)
        dve.wait_ge(self.h_turned, START + n)
        dve.tensor_tensor(self.buf.h[:], self.buf.silu[:], self.buf.p_u[:], ALU.mult).then_inc(self.h_ok, 1)

    def turn_h(self, pe, n):
        pe.wait_ge(self.h_ok, START + n + 1)
        pe.wait_ge(self.ht_moved, START + n)
        for k in range(KE):
            last = pe.transpose(self.buf.p_h[:, k, :], self.buf.h[:, k * P:(k + 1) * P], self.s.ident[:])
        last.then_inc(self.h_turned, 1)

    def move_h(self, act, n):
        act.wait_ge(self.h_turned, START + n + 1)
        act.wait_ge(self.downs, START + n)
        act.activation(self.buf.ht[:], self.buf.p_h[:], ACT.Copy).then_inc(self.ht_moved, 1)

    def down(self, pe, n, b, it):
        pe.wait_ge(self.ht_moved, START + n + 1)
        pe.wait_ge(self.d_in[b], (it + 1) * 16)
        pe.wait_ge(self.y_ok, START + n)
        for h in range(2):
            for k in range(KE):
                last = pe.matmul(self.buf.p_y[:, h, :], self.buf.ht[:, k, :], self.buf.wd[b][:, k, h * 512:(h + 1) * 512],
                                 start=(k == 0), stop=(k == KE - 1))
        last.then_inc(self.downs, 1)

    def move_y(self, dve, n, b, it):
        dve.wait_ge(self.downs, START + n + 1)
        dve.wait_ge(self.sid_in[b], (it + 1) * 16)
        dve.scalar_tensor_tensor(self.buf.y[b][:].rearrange("p (c n) -> p c n", c=2), self.buf.p_y[:], self.buf.sid[b][:, 2:3].bitcast(F32),
                                 self.s.gate2[:].rearrange("p (c n) -> p c n", c=2), ALU.mult, ALU.mult).then_inc(self.y_ok, 1)


def experts(nc, a, s):
    with ExitStack() as stack:
        t = Mem(nc, stack)
        buf = Buffers()
        buf.wg = [t.sb(f"wg{b}", [P, KD, DE]) for b in range(2)]
        buf.wu = [t.sb(f"wu{b}", [P, KD, DE]) for b in range(2)]
        buf.wd = [t.sb(f"wd{b}", [P, KE, D]) for b in range(2)]
        buf.sid = [t.sb(f"sid{b}", [CAP, 4], I32) for b in range(2)]
        buf.xg = [t.sb(f"xg{b}", [CAP, D]) for b in range(2)]
        buf.xt = [t.sb(f"xt5{b}", [P, KD, CAP]) for b in range(2)]
        buf.y = [t.sb(f"y5{b}", [CAP, D]) for b in range(2)]
        buf.silu, buf.h, buf.ht = t.sb("silu", [CAP, DE]), t.sb("h5", [CAP, DE]), t.sb("ht5", [P, KE, CAP])
        buf.p_x = [t.ps(f"p_x{b}", [P, 4, CAP]) for b in range(2)]
        buf.p_g, buf.p_u = t.ps("p_g", [CAP, DE]), t.ps("p_u", [CAP, DE])
        buf.p_h, buf.p_y = t.ps("p_h", [P, KE, CAP]), t.ps("p_y5", [CAP, 2, 512])
        q = ExpertSteps(t, a, s, buf, "first")
        o = ExpertSteps(t, a, s, buf, "over")
        xg_zero = t.sem("xg_zero")
        LAST = NE // 2 - 1

        def run(engine, body):
            with engine.Fori(0, LAST) as it:
                for b in range(2):
                    body(it * 2 + b, b, it, True)
            for b in range(2):
                body(LAST * 2 + b, b, LAST, b == 0)

        with nc.Block() as block:

            @block.sync
            def _(sp):
                for b in range(2):
                    q.load_slots(sp, b, b)
                    q.load_gate_up(sp, b, b)
                    q.load_down(sp, b, b)
                with sp.Fori(0, LAST) as it:
                    for b in range(2):
                        n = it * 2 + b
                        sp.wait_ge(q.gateups, START + n + 1)
                        sp.sem_inc(q.sp_passed, 1)
                        q.load_gate_up(sp, b, n + 2)
                        sp.wait_ge(q.downs, START + n + 1)
                        sp.sem_inc(q.sp_passed, 1)
                        q.load_down(sp, b, n + 2)
                        sp.wait_ge(q.scattered[b], (it + 1) * 16)
                        sp.sem_inc(q.sp_passed, 1)
                        q.load_slots(sp, b, n + 2)

            @block.gpsimd
            def _(pool):
                for sem in q.primed() + o.primed():
                    pool.sem_inc(sem, START)
                for b in range(2):
                    pool.memset(buf.xg[b][:], 0.0).then_inc(xg_zero, 1)
                pool.wait_ge(xg_zero, 2)
                q.gather(pool, 0, 0, 0)

                def body(n, b, it, more):
                    if more:
                        q.gather(pool, 1 - b, it + b, n)
                    q.scatter(pool, n, b)

                run(pool, body)
                for b in range(2):
                    pool.wait_ge(q.scattered[b], 16 * (NE // 2))

            @block.scalar
            def _(act):
                q.move_x(act, 0, 0, 0)

                def body(n, b, it, more):
                    q.silu(act, n)
                    if more:
                        q.move_x(act, n + 1, 1 - b, n)
                    q.move_h(act, n)

                run(act, body)

            @block.vector
            def _(dve):
                q.move_x(dve, 0, 0, 0)

                def body(n, b, it, more):
                    q.multiply(dve, n)
                    if more:
                        q.move_x(dve, n + 1, 1 - b, n)
                    q.move_y(dve, n, b, it)

                run(dve, body)

            @block.tensor
            def _(pe):
                q.turn_x(pe, 0, 0, 0)

                def body(n, b, it, more):
                    q.gate_up(pe, n, b, it)
                    if more:
                        q.turn_x(pe, n + 1, 1 - b, it + b)
                    q.turn_h(pe, n)
                    q.down(pe, n, b, it)

                run(pe, body)

        def each(engine, body):
            count = engine.value_load(s.blocks[0:1, OVB:OVB + 1], min_val=0, max_val=OVB)
            with engine.If(count > 0):
                with engine.Fori(0, count) as n:
                    body(n)

        with nc.Block() as block:

            @block.sync
            def _(sp):
                def body(n):
                    e = sp.value_load(s.blocks[0:1, bass.ds(n, 1)], min_val=0, max_val=NE - 1)
                    o.load_slots(sp, 0, n + NE)
                    o.load_gate_up(sp, 0, e)
                    o.load_down(sp, 0, e)
                    sp.wait_ge(o.scattered[0], (n + 1) * 16)
                    sp.sem_inc(o.sp_passed, 1)

                each(sp, body)

            @block.gpsimd
            def _(pool):
                def body(n):
                    o.gather(pool, 0, n, n)
                    o.scatter(pool, n, 0)
                    pool.wait_ge(o.scattered[0], (n + 1) * 16)
                    pool.sem_inc(o.passed, 1)

                each(pool, body)

            @block.scalar
            def _(act):
                def body(n):
                    o.move_x(act, n, 0, n)
                    o.silu(act, n)
                    o.move_h(act, n)

                each(act, body)

            @block.vector
            def _(dve):
                def body(n):
                    o.move_x(dve, n, 0, n)
                    o.multiply(dve, n)
                    o.move_y(dve, n, 0, n)

                each(dve, body)

            @block.tensor
            def _(pe):
                def body(n):
                    o.turn_x(pe, n, 0, n)
                    o.gate_up(pe, n, 0, n)
                    o.turn_h(pe, n)
                    o.down(pe, n, 0, n)

                each(pe, body)


def finish(nc, a, s):
    with ExitStack() as stack:
        t = Mem(nc, stack)
        yy = [t.sb(f"yy{b}", [P, 2, D]) for b in range(4)]
        junk = t.sb("junk6", [P, D])
        gain = t.sb("gain", [1, D])
        gains = t.sb("gains", [P, D])
        onerow, epsb = t.sb("onerow6", [1, P]), t.sb("epsb6", [P, 1])
        ss, root, rstd, tmp = (t.sb(n, [P, NT]) for n in ("ss6", "root6", "rstd6", "tmp6"))
        p_g = t.ps("p_g6", [P, 2, 512])
        y_in = [t.sem(f"y_in{b}") for b in range(4)]
        g_in, consts, spread, spread_ok = t.sem("g_in"), t.sem("consts6"), t.sem("spread"), t.sem("spread_ok")
        summed, squared, rooted, scaled, stored, chain = (t.sem(n) for n in ("summed6", "squared6", "rooted6", "scaled6", "stored", "chain6"))

        with nc.Block() as block:

            @block.sync
            def _(sp):
                sp.dma_start(gain[:], a.g_final).then_inc(g_in, 16)
                for i in range(NT):
                    if i >= 4:
                        sp.wait_ge(summed, 2 * (i - 3))
                    src = a.y_rows.rearrange("(c n) d -> n c d", c=2)[i * P:(i + 1) * P]
                    sp.dma_start(yy[i % 4][:], src).then_inc(y_in[i % 4], 16)

            @block.gpsimd
            def _(pool):
                pool.memset(onerow[:], 1.0).then_inc(consts, 1)
                pool.memset(epsb[:], EPS).then_inc(consts, 1)

            @block.tensor
            def _(pe):
                pe.wait_ge(consts, 2)
                pe.wait_ge(g_in, 16)
                for h in range(2):
                    last = pe.matmul(p_g[:, h, :], onerow[:], gain[:, h * 512:(h + 1) * 512], start=True, stop=True)
                last.then_inc(spread, 1)

            @block.scalar
            def _(act):
                act.wait_ge(spread, 1)
                act.activation(gains[:].rearrange("p (c n) -> p c n", c=2), p_g[:], ACT.Copy).then_inc(spread_ok, 1)
                act.wait_ge(consts, 2)
                for i in range(NT):
                    act.wait_ge(summed, 2 * (i + 1))
                    act.wait_ge(squared, i)
                    act.activation(junk[:], s.x1[:, i, :], ACT.Square, accum_out=ss[:, i:i + 1]).then_inc(squared, 1)
                    act.wait_ge(squared, i + 1)
                    act.activation(root[:, i:i + 1], ss[:, i:i + 1], ACT.Sqrt, scale=1.0 / D, bias=epsb[:, 0:1]).then_inc(rooted, 1)
                for i in range(NT):
                    act.wait_ge(scaled, i + 1)
                    act.dma_start(a.out[i * P:(i + 1) * P, :], s.x1[:, i, :]).then_inc(stored, 16)
                act.wait_ge(stored, 16 * NT)

            @block.vector
            def _(dve):
                c = Counter(dve, chain)

                def add(i):
                    dve.wait_ge(y_in[i % 4], 16 * (i // 4 + 1))
                    x1 = s.x1[:, i, :]
                    for k in range(2):
                        dve.tensor_tensor(x1, x1, yy[i % 4][:, k, :], ALU.add).then_inc(summed, 1)
                        if k == 0:
                            dve.wait_ge(summed, 2 * i + 1)

                def scale(i):
                    one = slice(i, i + 1)
                    dve.wait_ge(rooted, i + 1)
                    c.step(dve.reciprocal(rstd[:, one], root[:, one]))
                    newton(dve, c, rstd[:, one], ss[:, one], tmp[:, one], D, n=1)
                    dve.wait_ge(spread_ok, 1)
                    x1 = s.x1[:, i, :]
                    dve.scalar_tensor_tensor(x1, x1, rstd[:, one], gains[:], ALU.mult, ALU.mult).then_inc(scaled, 1)

                for i in range(NT):
                    add(i)
                    if i >= 1:
                        scale(i - 1)
                scale(NT - 1)


def build(nc, arrays, out):
    a = Arrays(arrays)
    a.out = out
    a.h_rows = nc.dram_tensor("h_rows", (N, D), F32).ap()
    a.y_rows = nc.dram_tensor("y_rows", (2 * N, D), F32).ap()
    a.slot_rows = nc.dram_tensor("slot_rows", (SLOTS, 4), I32).ap()
    a.slot_blocks = a.slot_rows.rearrange("(b p) c -> b p c", p=CAP)
    a.v_rows = nc.dram_tensor("v_rows", (N, DN), F32).ap()
    with ExitStack() as stack:
        m = Mem(nc, stack)
        s = Buffers()
        s.ident = m.sb("ident", [P, P])
        s.ones = m.sb("ones", [P, P])
        s.vcol = m.sb("vcol", [P, a.vecs.shape[0]])
        s.cond = m.sb("cond", [P, 2 * KD])
        s.scale2 = m.sb("scale2", [P, KD])
        s.shift2 = m.sb("shift2", [P, KD])
        s.gate1 = m.sb("gate1", [P, D])
        s.gate2 = m.sb("gate2", [P, D])
        s.blocks = m.sb("blocks", [1, OVB + 1], I32)
        s.x1 = m.sb("x1", [P, NT, D])
        s.fout = m.sb("fout", [P, NT, DF])
        with ExitStack() as mixer:
            mm = Mem(nc, mixer)
            s.ht = mm.sb("ht", [P, KD, N + L])
            s.vctx = mm.sb("vctx", [P, 2, DN])
            norm_inputs(nc, mm, a, s)
            project_values(nc, mm, a, s)
            s.na = mm.sb("na", [P, NT, DN])
            attention(nc, mm, a, s)
            mix_and_route(nc, mm, a, s)
        s.act = nc.scalar
        experts(nc, a, s)
        finish(nc, a, s)


def query_order(x):
    g = x.reshape(2, QR, 4, QC, *x.shape[1:]).swapaxes(1, 2)
    return np.ascontiguousarray(g[:, :, ::-1, ::-1].reshape(x.shape))


def grid_order(x):
    g = x.reshape(2, 4, QR, QC, *x.shape[1:])[:, :, ::-1, ::-1].swapaxes(1, 2)
    return np.ascontiguousarray(g.reshape(x.shape))


def bf16_bits(x):
    return (x.view(np.uint32) >> 16).astype(np.uint16)


def shape_constants():
    c = {"ident": np.eye(P, dtype=np.float32)}
    w = HD
    ang = 2 * np.pi * (np.outer(np.arange(w), np.arange(w)) % w) / w
    norm = 1.0 / np.sqrt(N * w)
    c["chan"] = np.stack([np.kron(np.eye(2), f(ang) * norm) for f in (np.cos, np.sin)]).astype(np.float32)
    pos = query_order(np.arange(N))
    ang = 2 * np.pi * (np.outer(np.arange(N), pos) % N) / N
    d = np.stack([np.cos(ang), -np.sin(ang)], axis=1).reshape(N, 2, NT, P)
    c["dft"] = np.ascontiguousarray(d.transpose(2, 0, 1, 3).astype(np.float32))
    half = HD // 4
    inv = 10000.0 ** (-np.arange(half, dtype=np.float32) / half)
    tok = np.arange(N)
    ch = np.arange(P) % HD
    where = np.where((ch < HD // 2)[:, None], (tok // GW)[None], (tok % GW)[None]).astype(np.float32)
    ang = where * inv[ch % half][:, None].astype(np.float32)
    c["rope"] = np.stack([np.cos(ang), np.sin(ang)]).astype(np.float32)
    rot = np.zeros((P, P), np.float32)
    for i in range(P):
        if i % (2 * half) < half:
            rot[i + half, i] = -1.0
        else:
            rot[i - half, i] = 1.0
    c["rot"] = rot
    mask = np.zeros((2, 4, P, KR, KC), np.float32)
    for h in range(2):
        for j in range(4):
            for p in range(P):
                r, q = QR * h + QR - 1 - p // QC, QC * j + QC - 1 - p % QC
                r0, c0 = min(max(r - 4, 0), 8), min(max(q - 8, 0), 48)
                kr, kc = 4 * h + np.arange(KR), COL0[j] + np.arange(KC)
                ok = ((kr >= r0) & (kr < r0 + 8))[:, None] & ((kc >= c0) & (kc < c0 + 16))[None]
                mask[h, j, p] = np.where(ok, 0.0, NEG)
    c["mask"] = bf16_bits(np.ascontiguousarray(mask.reshape(8, P, LOC).transpose(1, 0, 2)))
    c["before"] = np.triu(np.ones((P, P), np.float32), 1)
    c["desc"] = np.broadcast_to(np.arange(EPG, 0, -1, dtype=np.float32), (P, NT, EPG)).copy()
    c["base"] = np.broadcast_to(np.arange(NE, dtype=np.float32) * CAP, (P, NE)).copy()
    c["blk"] = np.broadcast_to(np.arange(OVB, dtype=np.float32)[:, None], (1, OVB, NE)).copy()
    tok = np.arange(N, dtype=np.int32).reshape(NT, P).T
    c["ids"] = np.stack([np.stack([tok, tok + k * N, 0 * tok, 0 * tok], axis=-1) for k in range(2)], axis=1).astype(np.int32)
    c["eye16"] = bf16_bits(np.eye(P, dtype=np.float32))
    return c


def host_layout(x, c, ctx, c_ctx, w_ada, b_ada, g_norm1, w_in, w_fmix, rpb, g_out, w_out, g_norm2,
                w_router_group, w_router_expert, w_gate, w_up, w_down, g_final):
    h = {k: np.asarray(v) for k, v in dict(
        x=x, c=c, ctx=ctx, c_ctx=c_ctx, w_ada=w_ada, b_ada=b_ada, g_norm1=g_norm1, w_in=w_in, w_fmix=w_fmix, rpb=rpb,
        g_out=g_out, w_out=w_out, g_norm2=g_norm2, wrg=w_router_group, wre=w_router_expert, w_gate=w_gate,
        w_up=w_up, w_down=w_down, g_final=g_final).items()}
    out = shape_constants()
    out["vecs"] = np.concatenate([h[k].reshape(-1, P) for k in ("b_ada", "c", "c_ctx", "g_norm1", "g_norm2", "g_out")])
    out["x_nat"] = h["x"].reshape(N, D)
    out["x_perm"] = query_order(h["x"].reshape(N, D))
    out["ctx"] = h["ctx"].reshape(L, D)
    for k in ("w_ada", "w_in", "w_fmix", "w_out", "w_gate", "w_up", "w_down"):
        out[k] = h[k].reshape(h[k].shape[1:])
    out["b_ada"] = h["b_ada"]
    rows = np.zeros((NH, RPB), np.float32)
    body = np.zeros((NH, 15, PITCH), np.float32)
    body[:, :, 0:31] = h["rpb"][0]
    rows[:, LEAD:LEAD + 15 * PITCH] = body.reshape(NH, -1)
    out["rpb"] = rows
    out["w_router"] = np.concatenate([h["wrg"][0], h["wre"][0]], axis=1)
    out["g_final"] = h["g_final"].reshape(1, D)
    return out


def kernel(**inputs):
    import concourse.bacc as bacc
    from concourse.bass_utils import run_bass_kernel_spmd

    arrays = {f"in_{k}": v for k, v in host_layout(**inputs).items()}
    nc = bacc.Bacc("TRN2", target_bir_lowering=False, num_devices=1)
    aps = {k[3:]: nc.dram_tensor(k, v.shape, mybir.dt.from_np(v.dtype), kind="ExternalInput").ap() for k, v in arrays.items()}
    out = nc.dram_tensor("out", (N, D), F32, kind="ExternalOutput").ap()
    build(nc, aps, out)
    r = run_bass_kernel_spmd(nc, [arrays], core_ids=[0])
    return grid_order(r.results[0]["out"]).reshape(1, N, D)
```

```python
from contextlib import ExitStack

import numpy as np

import concourse.bass as bass
from concourse import mybir

F32 = mybir.dt.float32
F32R = mybir.dt.float32r
BF16 = mybir.dt.bfloat16
I32 = mybir.dt.int32
ALU = mybir.AluOpType
ACT = mybir.ActivationFunctionType
AX = mybir.AxisListType

P = 128
D = 1024
KD = D // P
N = 1024
NT = N // P
L = 256
GW = 64
HD = 64
NH = 12
HP = NH // 2
DF = 256
DN = NH * HD
NG = 4
NE = 32
EPG = NE // NG
DE = 512
KE = DE // P
EPS = 1e-6

QR, QC, KR, KC = 8, 16, 12, 32
LOC = KR * KC
KEYS = LOC + L
COL0 = [0, 8, 24, 32]
KIND = [0, 1, 1, 2]
PITCH = 32
LEAD = 144
RPB = 768
NEG = -1.0e30
LOWEST = -3.0e38

START = 1
CAP = P
OVB = 16
SLOTS = (NE + OVB) * CAP
CHUNKS, CHUNK = 6, 2048
POOL_LOWS = (3,)
RING = 4
SKIP = 1 << 20


class Counter:

    def __init__(self, engine, sem, base=0):
        self.engine, self.sem, self.base, self.n = engine, sem, base, 0

    def step(self, instruction):
        instruction.then_inc(self.sem, 1)
        self.n += 1
        self.engine.wait_ge(self.sem, self.base + self.n)


class Buffers:
    pass


class Arrays:

    def __init__(self, d):
        self.vecs, self.b_ada, self.w_ada, self.x_nat, self.x_perm, self.ctx = d["vecs"], d["b_ada"], d["w_ada"], d["x_nat"], d["x_perm"], d["ctx"]
        self.w_in, self.w_fmix, self.w_out, self.w_router, self.rpb = d["w_in"], d["w_fmix"], d["w_out"], d["w_router"], d["rpb"]
        self.w_gate, self.w_up, self.w_down, self.g_final = d["w_gate"], d["w_up"], d["w_down"], d["g_final"]
        self.ident, self.chan, self.dft, self.rope, self.rot, self.mask = (
            d["ident"], d["chan"], d["dft"], d["rope"], d["rot"], d["mask"])
        self.before, self.desc, self.base, self.blk, self.ids = d["before"], d["desc"], d["base"], d["blk"], d["ids"]


class Mem:

    def __init__(self, nc, stack):
        self.nc, self.stack = nc, stack

    def sb(self, name, shape, dt=F32):
        return self.stack.enter_context(self.nc.sbuf_tensor(name, shape, dt))

    def ps(self, name, shape, dt=F32):
        return self.stack.enter_context(self.nc.psum_tensor(name, shape, dt))

    def sem(self, name):
        return self.stack.enter_context(self.nc.semaphore(name))


def norm_inputs(nc, m, a, s):
    with ExitStack() as stack:
        t = Mem(nc, stack)
        rows = a.vecs.shape[0]
        vrow = t.sb("vrow", [rows, P])
        wa = [t.sb(f"wa{b}", [P, KD, D]) for b in range(2)]
        xc = t.sb("xc", [P, 2, D])
        xt = [s.x1[:, i, :] for i in range(NT)] + [xc[:, i, :] for i in range(2)]
        acc = [s.raw[b][:, 0:D] for b in range(4)]
        junk = t.sb("junk", [P, D])
        ss = t.sb("ss", [P, 10])
        root = t.sb("root", [P, 10])
        rstd = t.sb("rstd", [P, 10])
        tmp = t.sb("tmp", [P, 10])
        part = t.sb("part", [P, 2, KD])
        cols = t.sb("cols", [P, 4, KD])
        one = t.sb("one", [P, 1])
        epsb = t.sb("epsb", [P, 1])
        p_v = t.ps("p_v", [P, 512])
        p_c = t.ps("p_c", [P, 512])
        p_t = [t.ps(f"p_t{b}", [P, 512]) for b in range(4)]

        vecs_in, x_in, w_in = t.sem("vecs_in"), [t.sem(f"x_in{g}") for g in range(3)], [t.sem(f"wa_in{b}") for b in range(8)]
        vecs_t, vecs_ok, silu_ok = t.sem("vecs_t"), t.sem("vecs_ok"), t.sem("silu_ok")
        accs, sums, mods = t.sem("accs"), t.sem("sums"), t.sem("mods")
        squares, roots, rstds, normed = t.sem("squares"), t.sem("roots"), t.sem("rstds"), t.sem("normed")
        turned, moved_a, moved_v, consts_ok = t.sem("turned"), t.sem("moved_a"), t.sem("moved_v"), t.sem("consts_ok")
        dchain = t.sem("dchain")
        groups = [(0, 4), (4, 4), (8, 2)]

        with nc.Block() as block:

            @block.sync
            def _(sp):
                sp.dma_start(vrow[:], a.vecs).then_inc(vecs_in, 16)
                sp.dma_start(s.ident[:], a.ident).then_inc(vecs_in, 16)

                def weights(j, q):
                    src = a.w_ada[2 * q * P:2 * (q + 1) * P, j * D:(j + 1) * D]
                    sp.dma_start(wa[j][:, 2 * q:2 * q + 2, :], src.rearrange("(k p) n -> p k n", p=P)).then_inc(w_in[4 * j + q], 16)

                def latents(g):
                    src = a.x_nat[g * 512:(g + 1) * 512, :]
                    sp.dma_start(s.x1[:, 4 * g:4 * g + 4, :], src.rearrange("(t p) n -> p t n", p=P)).then_inc(x_in[g], 16)

                for q in range(4):
                    weights(0, q)
                latents(0)
                weights(1, 0)
                weights(1, 1)
                latents(1)
                weights(1, 2)
                sp.dma_start(xc[:], a.ctx.rearrange("(t p) n -> p t n", p=P)).then_inc(x_in[2], 16)
                weights(1, 3)

            @block.gpsimd
            def _(pool):
                pool.memset(s.ones[:], 1.0).then_inc(consts_ok, 1)
                pool.memset(one[:], 1.0).then_inc(consts_ok, 1)
                pool.memset(epsb[:], EPS).then_inc(consts_ok, 1)

            @block.scalar
            def _(act):
                act.wait_ge(vecs_ok, 1)
                act.activation(s.cond[:], s.vcol[:, 48:64], ACT.Silu).then_inc(silu_ok, 1)
                for g, (t0, n) in enumerate(groups):
                    act.wait_ge(x_in[g], 16)
                    for i in range(t0, t0 + n):
                        act.wait_ge(squares, i)
                        act.activation(junk[:], xt[i], ACT.Square, accum_out=ss[:, i:i + 1]).then_inc(squares, 1)
                    if g >= 1:
                        part_ = slice(0, 8) if g == 1 else slice(8, 10)
                        act.wait_ge(squares, t0 + n)
                        act.wait_ge(consts_ok, 3)
                        act.activation(root[:, part_], ss[:, part_], ACT.Sqrt, scale=1.0 / D, bias=epsb[:, 0:1]).then_inc(roots, 1)
                for i in range(10):
                    act.wait_ge(rstds, 1 if i < 8 else 2)
                    act.activation(xt[i], xt[i], ACT.Copy, scale=rstd[:, i:i + 1]).then_inc(normed, 1)
                act.wait_ge(mods, 4)
                u = 0
                for g, (t0, n) in enumerate(groups):
                    sh, sc = (0, 1) if g < 2 else (2, 3)
                    for k in range(KD):
                        if u % 2 == 0:
                            act.wait_ge(turned, u + 1)
                            act.activation(s.ht[:, k, t0 * P:(t0 + n) * P], p_t[u % 4][:, 0:n * P], ACT.Identity,
                                           scale=cols[:, sc, k:k + 1], bias=cols[:, sh, k:k + 1]).then_inc(moved_a, 1)
                        u += 1

            @block.vector
            def _(dve):
                c = Counter(dve, dchain)
                dve.wait_ge(vecs_t, 1)
                dve.tensor_copy(s.vcol[:], p_v[:, 0:rows]).then_inc(vecs_ok, 1)
                dve.wait_ge(silu_ok, 1)
                n = 0

                def inverse_roots(part_, count):
                    dve.wait_ge(roots, count)
                    c.step(dve.reciprocal(rstd[:, part_], root[:, part_]))
                    newton(dve, c, rstd[:, part_], ss[:, part_], tmp[:, part_], D, n=1)
                    dve.sem_inc(rstds, 1)

                for j in range(2):
                    for k in range(KD):
                        if k % 2 == 0:
                            if j == 1 and k == 6:
                                inverse_roots(slice(0, 8), 1)
                            dve.wait_ge(w_in[4 * j + k // 2], 16)
                        for w in range(2):
                            dst = acc[2 * w + j]
                            cc = s.cond[:, 8 * w + k:8 * w + k + 1]
                            if k == 0:
                                dve.tensor_scalar(dst[:], wa[j][:, k, :], cc, None, ALU.mult).then_inc(accs, 1)
                            else:
                                dve.wait_ge(accs, n - 1)
                                dve.scalar_tensor_tensor(dst[:], wa[j][:, k, :], cc, dst[:], ALU.mult, ALU.add).then_inc(accs, 1)
                            n += 1
                inverse_roots(slice(8, 10), 2)
                dve.wait_ge(sums, 2)
                for w in range(2):
                    dve.tensor_tensor(cols[:, 2 * w, :], p_c[:, 16 * w:16 * w + 8], s.vcol[:, 0:8], ALU.add).then_inc(mods, 1)
                    c.step(dve.tensor_tensor(part[:, w, :], p_c[:, 16 * w + 8:16 * w + 16], s.vcol[:, 8:16], ALU.add))
                    dve.scalar_tensor_tensor(cols[:, 2 * w + 1, :], part[:, w, :], 1.0, s.vcol[:, 64:72], ALU.add, ALU.mult).then_inc(mods, 1)
                dve.wait_ge(mods, 4)
                u = 0
                for g, (t0, n_) in enumerate(groups):
                    sh, sc = (0, 1) if g < 2 else (2, 3)
                    for k in range(KD):
                        if u % 2 == 1:
                            dve.wait_ge(turned, u + 1)
                            dve.tensor_scalar(s.ht[:, k, t0 * P:(t0 + n_) * P], p_t[u % 4][:, 0:n_ * P],
                                              cols[:, sc, k:k + 1], cols[:, sh, k:k + 1], ALU.mult, ALU.add).then_inc(moved_v, 1)
                        u += 1

            @block.tensor
            def _(pe):
                pe.wait_ge(vecs_in, 32)
                pe.transpose(p_v[:, 0:rows], vrow[:], s.ident[0:rows, 0:rows]).then_inc(vecs_t, 1)

                def modulation(j):
                    pe.wait_ge(accs, 16 * (j + 1))
                    for b in (j, 2 + j):
                        for k in range(KD):
                            last = pe.matmul(p_c[:, 8 * b + k:8 * b + k + 1], acc[b][:, k * P:(k + 1) * P], one[:], start=True, stop=True)
                    last.then_inc(sums, 1)

                pe.wait_ge(consts_ok, 3)
                modulation(0)
                u = 0
                for g, (t0, n) in enumerate(groups):
                    pe.wait_ge(normed, t0 + n)
                    for k in range(KD):
                        if u == 4:
                            modulation(1)
                        if u >= 4:
                            pe.wait_ge(moved_a if u % 2 == 0 else moved_v, (u - 4) // 2 + 1)
                        for i in range(n):
                            last = pe.transpose(p_t[u % 4][:, i * P:(i + 1) * P], xt[t0 + i][:, k * P:(k + 1) * P], s.ident[:])
                        last.then_inc(turned, 1)
                        u += 1


def newton(dve, c, r, ss, tmp, width, n=None):
    rr, tt, sq = (r[:], tmp[:], ss[:]) if n is None else (r, tmp, ss)
    c.step(dve.tensor_tensor(tt, rr, rr, ALU.mult))
    c.step(dve.tensor_scalar(sq, sq, 1.0 / width, EPS, ALU.mult, ALU.add))
    c.step(dve.tensor_tensor(tt, tt, sq, ALU.mult))
    c.step(dve.tensor_scalar(tt, tt, -0.5, 1.5, ALU.mult, ALU.add))
    c.step(dve.tensor_tensor(rr, rr, tt, ALU.mult))


def project_values(nc, m, a, s):
    with ExitStack() as stack:
        t = Mem(nc, stack)
        wv = t.sb("wv", [P, KD, DN])
        wf = t.sb("wf", [P, KD, DF])
        vrow = [t.sb(f"v_row{b}", [P, DN]) for b in range(2)]
        fmix = t.sb("fmix", [P, 2, DF])
        chan = t.sb("chan", [P, 2, P])
        ab = t.sb("ab", [P, 2, 2 * DF])
        gg = s.x1[:, 0:2, :].rearrange("p a (b n) -> p (a b) n", b=2)
        ft = s.x1[:, 4:6, :]
        dft = [s.raw[b][:, 0:NT * P].rearrange("p (n c m) -> p n c m", n=NT // 2, c=2) for b in range(2)]
        half = N // 2
        plus, minus = (s.raw[2][:, w * N:(w + 1) * N].rearrange("p (c n) -> p c n", c=2) for w in range(2))
        middle = s.raw[3][:, 0:2 * P].rearrange("p (c n) -> p c n", c=2)
        wa = [t.sb(f"wa2{b}", [P, 2, D]) for b in range(2)]
        acc = [t.sb(f"acc2{b}", [P, D]) for b in range(2)]
        brow = t.sb("brow", [1, 2, D])
        onerow = t.sb("onerow", [1, P])
        tmp = t.sb("tmp2", [P, KD])
        p_v = [t.ps(f"p_v{b}", [P, 2, 512]) for b in range(2)]
        p_f = [t.ps(f"p_f{b}", [P, 512]) for b in range(2)]
        p_m = t.ps("p_m", [P, 2, 512])

        wv_in = [t.sem(f"wv_in{h}") for h in range(2)]
        wf_in, fm_in = t.sem("wf_in"), t.sem("fm_in")
        wa_in = [t.sem(f"wa2_in{b}") for b in range(2)]
        dft_in = [t.sem(f"dft_in{b}") for b in range(2)]
        v_out = [t.sem(f"v_out{b}") for b in range(2)]
        values, values_moved = t.sem("values"), t.sem("values_moved")
        four, four_moved = t.sem("four"), t.sem("four_moved")
        accs, modsum, modmoved, chain = t.sem("accs2"), t.sem("modsum"), t.sem("modmoved"), t.sem("chain2")

        folded = t.sem("folded")
        AB, FT, G = 2, 6, 10
        with nc.Block() as block:

            @block.sync
            def _(sp):
                for h in range(2):
                    c0 = DF + 2 * DN + h * DN // 2
                    sp.dma_start(wv[:, :, h * DN // 2:(h + 1) * DN // 2],
                                 a.w_in[:, c0:c0 + DN // 2].rearrange("(k p) n -> p k n", p=P)).then_inc(wv_in[h], 16)
                sp.dma_start(wf[:], a.w_in[:, 0:DF].rearrange("(k p) n -> p k n", p=P)).then_inc(wf_in, 16)
                sp.dma_start(fmix[:], a.w_fmix.rearrange("(k p) n -> p k n", p=P)).then_inc(fm_in, 16)
                sp.dma_start(chan[:], a.chan.rearrange("c p n -> p c n")).then_inc(fm_in, 16)
                sp.dma_start(brow[:, 0, :], a.b_ada[:, 2 * D:3 * D]).then_inc(fm_in, 16)
                sp.dma_start(brow[:, 1, :], a.b_ada[:, 5 * D:6 * D]).then_inc(fm_in, 16)
                for b in range(2):
                    sp.dma_start(dft[b][:], a.dft[b].rearrange("(n p) c m -> p n c m", p=P)).then_inc(dft_in[b], 16)
                for u in range(16):
                    j, k = 2 + u // 4, 2 * (u % 4)
                    if u >= 2:
                        sp.wait_ge(accs, 2 * (u - 1))
                    src = a.w_ada[k * P:(k + 2) * P, j * D:(j + 1) * D]
                    sp.dma_start(wa[u % 2][:], src.rearrange("(k p) n -> p k n", p=P)).then_inc(wa_in[u % 2], 16)
                for i in range(2, NT):
                    sp.wait_ge(four, G + i - 1)
                    sp.dma_start(dft[i % 2][:], a.dft[i].rearrange("(n p) c m -> p n c m", p=P)).then_inc(dft_in[i % 2], 16)

            @block.gpsimd
            def _(pool):
                pool.memset(onerow[:], 1.0).then_inc(folded, 1)
                pool.memset(middle, 0.0).then_inc(folded, 1)
                pool.wait_ge(folded, 2)
                for c in range(2):
                    pool.wait_ge(four_moved, AB + 2 * (c + 1))
                    fwd, back = ft[:, c, 1:half], ft[:, c, half + 1:N][:, ::-1]
                    pool.tensor_tensor(plus[:, c, 1:half], fwd, back, ALU.add).then_inc(folded, 1)
                    pool.tensor_tensor(minus[:, c, 1:half], fwd, back, ALU.subtract).then_inc(folded, 1)
                    pool.tensor_copy(plus[:, c, 0:1], ft[:, c, 0:1]).then_inc(folded, 1)
                    pool.memset(minus[:, c, 0:1], 0.0).then_inc(folded, 1)
                    pool.tensor_copy(middle[:, c, 0:1], ft[:, c, half:half + 1]).then_inc(folded, 1)

            @block.scalar
            def _(act):
                def fourier(u):
                    act.wait_ge(four, u + 1)
                    src = p_f[u % 2]
                    if u < AB:
                        act.activation(ab[:, u, :], src[:], ACT.Copy).then_inc(four_moved, 1)
                    elif u < FT:
                        c_, h = (u - 2) // 2, (u - 2) % 2
                        act.activation(ft[:, c_, h * 512:(h + 1) * 512], src[:], ACT.Copy).then_inc(four_moved, 1)
                    elif u < G:
                        act.activation(gg[:, u - FT, :], src[:], ACT.Copy).then_inc(four_moved, 1)
                    else:
                        act.activation(s.fout[:, u - G, :], src[:, 0:DF], ACT.Copy).then_inc(four_moved, 1)

                for i in range(NT + 2):
                    act.wait_ge(values, i + 1)
                    if i >= 2 and i < NT:
                        act.wait_ge(v_out[i % 2], 16 * (i // 2))
                    dst = vrow[i % 2][:] if i < NT else s.vctx[:, i - NT, :]
                    act.activation(dst.rearrange("p (c n) -> p c n", c=2), p_v[i % 2][:, :, 0:DN // 2], ACT.Copy).then_inc(values_moved, 1)
                    if i < NT:
                        act.wait_ge(values_moved, i + 1)
                        act.dma_start(a.v_rows[i * P:(i + 1) * P, :], vrow[i % 2][:]).then_inc(v_out[i % 2], 16)
                for u in range(G + NT):
                    fourier(u)
                for b in range(2):
                    act.wait_ge(v_out[b], 16 * (NT // 2))

            @block.vector
            def _(dve):
                c = Counter(dve, chain)
                n = 0

                def modulation(u):
                    nonlocal n
                    j = u // 4
                    dve.wait_ge(wa_in[u % 2], 16 * (u // 2 + 1))
                    for k in (2 * (u % 4), 2 * (u % 4) + 1):
                        dst, cc = acc[j % 2], s.cond[:, k:k + 1]
                        if k == 0:
                            if j >= 2:
                                dve.wait_ge(modsum, j - 1)
                            dve.tensor_scalar(dst[:], wa[u % 2][:, k % 2, :], cc, None, ALU.mult).then_inc(accs, 1)
                        else:
                            dve.wait_ge(accs, n)
                            dve.scalar_tensor_tensor(dst[:], wa[u % 2][:, k % 2, :], cc, dst[:], ALU.mult, ALU.add).then_inc(accs, 1)
                        n += 1

                def modulation_out(j):
                    dve.wait_ge(modsum, j + 1)
                    if j == 0:
                        dve.tensor_copy(s.gate1[:].rearrange("p (c n) -> p c n", c=2), p_m[:]).then_inc(modmoved, 1)
                    if j == 3:
                        dve.tensor_copy(s.gate2[:].rearrange("p (c n) -> p c n", c=2), p_m[:]).then_inc(modmoved, 1)
                    if j == 1:
                        dve.tensor_tensor(s.shift2[:], p_m[:, 0, 0:KD], s.vcol[:, 24:32], ALU.add).then_inc(modmoved, 1)
                    if j == 2:
                        c.step(dve.tensor_tensor(tmp[:], p_m[:, 0, 0:KD], s.vcol[:, 32:40], ALU.add))
                        dve.scalar_tensor_tensor(s.scale2[:], tmp[:], 1.0, s.vcol[:, 72:80], ALU.add, ALU.mult).then_inc(modmoved, 1)

                for u in range(16):
                    modulation(u)
                    if u % 4 == 3 and u >= 7:
                        modulation_out(u // 4 - 1)
                modulation_out(3)

            @block.tensor
            def _(pe):
                def value_tile(i):
                    if i >= 2:
                        pe.wait_ge(values_moved, i - 1)
                    for h in range(2):
                        if i == 0:
                            pe.wait_ge(wv_in[h], 16)
                        for k in range(KD):
                            last = pe.matmul(p_v[i % 2][:, h, 0:DN // 2], s.ht[:, k, i * P:(i + 1) * P],
                                             wv[:, k, h * 384:(h + 1) * 384], start=(k == 0), stop=(k == KD - 1))
                    last.then_inc(values, 1)

                def modulation_sum(j):
                    pe.wait_ge(accs, 8 * (j + 1))
                    if j >= 1:
                        pe.wait_ge(modmoved, j)
                    src = acc[j % 2]
                    if j in (0, 3):
                        for h in range(2):
                            pe.matmul(p_m[:, h, :], s.ones[:], src[:, h * 512:(h + 1) * 512], start=True, stop=False)
                            last = pe.matmul(p_m[:, h, :], onerow[:], brow[:, j // 3, h * 512:(h + 1) * 512], start=False, stop=True)
                    else:
                        for k in range(KD):
                            last = pe.matmul(p_m[:, 0, k:k + 1], src[:, k * P:(k + 1) * P], s.ones[:, 0:1], start=True, stop=True)
                    last.then_inc(modsum, 1)

                def fourier(u):
                    if u >= 2:
                        pe.wait_ge(four_moved, u - 1)
                    dst = p_f[u % 2]
                    if u < AB:
                        for c in range(2):
                            last = pe.matmul(dst[:, c * DF:(c + 1) * DF], chan[:, c, :], fmix[:, u, :], start=True, stop=True)
                    elif u < FT:
                        c, h = (u - 2) // 2, (u - 2) % 2
                        for k in range(KD):
                            last = pe.matmul(dst[:], wf[:, k, c * P:(c + 1) * P], s.ht[:, k, h * 512:(h + 1) * 512],
                                             start=(k == 0), stop=(k == KD - 1))
                    elif u < G:
                        i = u - FT
                        pe.wait_ge(folded, 12)
                        rows = slice(i * P, (i + 1) * P)
                        for c in range(2):
                            pe.matmul(dst[:, 0:DF], plus[:, c, rows], ab[:, c, 0:DF], start=(c == 0), stop=(c == 1))
                        for c in range(2):
                            last = pe.matmul(dst[:, DF:], minus[:, c, rows], ab[:, c, DF:], start=(c == 0), stop=(c == 1 and i > 0))
                        if i == 0:
                            for c in range(2):
                                last = pe.matmul(dst[:, DF:], middle[:, c, :], ab[:, c, 0:DF], start=False, stop=(c == 1))
                    else:
                        i = u - G
                        pe.wait_ge(four_moved, G)
                        pe.wait_ge(dft_in[i % 2], 16 * (i // 2 + 1))
                        for n in range(NT // 2):
                            for c in range(2):
                                last = pe.matmul(dst[:, 0:DF], dft[i % 2][:, n, c, :], gg[:, n, c * DF:(c + 1) * DF],
                                                 start=(n + c == 0), stop=(n == NT // 2 - 1 and c == 1))
                    last.then_inc(four, 1)

                for i in range(NT + 2):
                    value_tile(i)
                pe.wait_ge(fm_in, 64)
                pe.wait_ge(wf_in, 16)
                pe.wait_ge(folded, 2)
                fourier(0)
                fourier(1)
                modulation_sum(0)
                for u in range(2, 6):
                    if u == 4:
                        modulation_sum(1)
                    fourier(u)
                modulation_sum(2)
                modulation_sum(3)
                for u in range(FT, G + NT):
                    fourier(u)


def attention(nc, m, a, s):
    PAIR = 2 * NT
    with ExitStack() as stack:
        t = Mem(nc, stack)
        rope = s.x1[:, 0:2, :]
        rot = t.sb("rot", [P, P])
        mask = t.sb("mask", [P, NT, LOC], BF16)
        wqk = t.sb("wqk", [P, KD, 2, P])
        vh = s.raw[2][:].rearrange("p (g n) -> p g n", g=16)
        plain = [s.raw[0][:, g * 512:(g + 1) * 512] for g in range(4)]
        turned = [s.raw[1][:, g * 512:(g + 1) * 512] for g in range(2)]
        cpart, spart = s.raw[1][:, 1024:1536], s.raw[1][:, 1536:2048]
        table = [t.sb(f"table{h}", [P, NT, LOC]) for h in range(2)]
        qwin = [s.x1[:, 2 + h, :] for h in range(2)]
        qctx = [s.x1[:, 4 + h, :] for h in range(2)]
        kwin, kctx = s.x1[:, 6, :], t.sb("kctx", [P, L])
        biased = [t.sb(f"biased{b}", [P, LOC]) for b in range(2)]
        prob = [t.sb(f"prob{b}", [P, KEYS]) for b in range(2)]
        probt = [t.sb(f"probt{b}", [P, KEYS]) for b in range(2)]
        cmax, rmax, nmax = t.sb("cmax", [P, PAIR]), t.sb("rmax", [P, PAIR]), t.sb("nmax", [P, PAIR])
        psum1, psum2, rsum = t.sb("psum1", [P, PAIR]), t.sb("psum2", [P, PAIR]), t.sb("rsum", [P, PAIR])
        p_win = [t.ps(f"p_win{b}", [P, 512]) for b in range(2)]
        p_ctx = [t.ps(f"p_ctx{b}", [P, 512]) for b in range(2)]
        p_t = [t.ps(f"p_tr{b}", [P, 512]) for b in range(2)]
        p_j, p_o = t.ps("p_j", [P, 512]), t.ps("p_o", [P, 512])

        const_in, zeroed = t.sem("const_in"), t.sem("zeroed")
        w_in, v_in, tab_in = t.sem("w_in3"), t.sem("v_in"), [t.sem(f"tab_in{h}") for h in range(2)]
        projected, proj_moved, rotated, roped, padded = (t.sem(n) for n in ("projected", "proj_moved", "rotated", "roped", "padded"))
        scored, maxed, exped, probs_t, pt_win, pt_ctx, weighted, normed = (
            t.sem(n) for n in ("scored", "maxed", "exped", "probs_t", "pt_win", "pt_ctx", "weighted", "normed3"))
        masked = [t.sem(f"masked{h}") for h in range(2)]
        biased_ok = [t.sem(f"biased_ok{h}") for h in range(2)]
        passed = t.sem("passed")
        chain, cmaxed = t.sem("chain3"), t.sem("cmaxed")

        with nc.Block() as block:

            @block.sync
            def _(sp):
                def pair_weights(hp):
                    for w in range(2):
                        src = a.w_in[:, bass.ds(DF + w * DN + hp * P, P)]
                        sp.dma_start(wqk[:, :, w, :], src.rearrange("(k p) n -> p k n", p=P)).then_inc(w_in, 16)

                pair_weights(0)
                for dst, src in ((rope, a.rope.rearrange("c p n -> p c n")), (rot[:], a.rot), (mask[:], a.mask.bitcast(BF16))):
                    sp.dma_start(dst, src).then_inc(const_in, 16)
                def tables_and_values(hp):
                    for h in range(2):
                        sp.wait_ge(biased_ok[h], START + hp * NT)
                        for i in range(NT):
                            first = LEAD - 128 * (i // 4) - 8 * KIND[i % 4]
                            src = bass.AP(a.rpb.tensor, (hp * 2 + h) * RPB + first, [[PITCH, QR], [1, QC], [1, LOC]])
                            sp.dma_start(table[h][:, i, :], src).then_inc(tab_in[h], 16)
                        if h == 0:
                            sp.wait_ge(weighted, START + hp * PAIR)
                            sp.sem_inc(passed, 1)
                            for j in range(4):
                                for g in range(4):
                                    src = a.v_rows[g * 4 * GW:(g + 1) * 4 * GW, bass.ds(hp * P, P)]
                                    src = src.rearrange("(r c) n -> r c n", c=GW)[:, COL0[j]:COL0[j] + KC, :]
                                    sp.dma_start(vh[:, 4 * j + g, :], src).then_inc(v_in, 16)

                with sp.Fori(0, HP - 1) as hp:
                    tables_and_values(hp)
                    sp.wait_ge(projected, START + (hp + 1) * 5)
                    sp.sem_inc(passed, 1)
                    pair_weights(hp + 1)
                tables_and_values(HP - 1)

            @block.gpsimd
            def _(pool):
                for sem in (projected, weighted, scored, proj_moved, roped, padded, probs_t, exped, pt_win, pt_ctx, normed, *biased_ok):
                    pool.sem_inc(sem, START)
                for h in range(2):
                    pool.memset(qwin[h], 0.0).then_inc(zeroed, 1)
                    pool.memset(qctx[h], 0.0).then_inc(zeroed, 1)
                pool.wait_ge(zeroed, 4)
                pool.wait_ge(const_in, 48)
                with pool.Fori(0, HP) as hp:
                    def add_mask(h):
                        pool.wait_ge(tab_in[h], (hp + 1) * 16 * NT)
                        pool.sem_inc(passed, 1)
                        pool.tensor_tensor(table[h][:], table[h][:], mask[:], ALU.add).then_inc(masked[h], 1)
                        pool.wait_ge(masked[h], hp + 1)
                        pool.sem_inc(passed, 1)

                    add_mask(0)
                    pool.wait_ge(scored, START + hp * PAIR)
                    for g in range(2):
                        pool.wait_ge(proj_moved, START + hp * 5 + g + 1)
                        pool.sem_inc(passed, 1)
                        for src, dst in ((plain[g], qctx), (turned[g], qwin)):
                            if src is turned[g]:
                                pool.wait_ge(roped, START + hp * 4 + g + 1)
                                pool.sem_inc(passed, 1)
                            for h in range(2):
                                rows = slice(HD * h, HD * h + HD)
                                grid = src[rows, :].rearrange("p (r j c) -> p j r c", r=QR, j=4)[:, :, ::-1, ::-1]
                                tile = dst[h][rows, g * 512:(g + 1) * 512].rearrange("p (j r c) -> p j r c", r=QR, j=4)
                                pool.tensor_copy(tile, grid).then_inc(padded, 1)
                    pool.wait_ge(padded, START + (hp + 1) * 8)
                    pool.sem_inc(passed, 1)
                    add_mask(1)

            @block.scalar
            def _(act):
                with act.Fori(0, HP) as hp:
                    for g in range(5):
                        act.wait_ge(projected, START + hp * 5 + g + 1)
                        if g == 0:
                            act.wait_ge(roped, START + hp * 4)
                            act.wait_ge(padded, START + hp * 8)
                            act.wait_ge(scored, START + hp * PAIR)
                        src = (p_j, p_o)[g % 2]
                        if g < 4:
                            act.activation(plain[g][:], src[:], ACT.Copy, scale=HD ** -0.5 if g < 2 else 1.0).then_inc(proj_moved, 1)
                        else:
                            act.activation(kctx[:], src[:, 0:L], ACT.Copy).then_inc(proj_moved, 1)
                    for n in range(PAIR + 1):
                        b = n % 2
                        if n < PAIR:
                            act.wait_ge(maxed, hp * PAIR + n + 1)
                            act.wait_ge(probs_t, START + hp * PAIR + max(n - 1, 0))
                            act.activation(prob[b][:, 0:LOC], biased[b][:], ACT.Exp, bias=nmax[:, n:n + 1],
                                           accum_out=psum1[:, n:n + 1])
                            act.activation(prob[b][:, LOC:KEYS], p_ctx[b][:, 0:L], ACT.Exp, bias=nmax[:, n:n + 1],
                                           accum_out=psum2[:, n:n + 1]).then_inc(exped, 1)
                        if n >= 1:
                            act.wait_ge(probs_t, START + hp * PAIR + n)
                            act.wait_ge(weighted, START + hp * PAIR + max(n - 2, 0))
                            act.activation(probt[1 - b][:, 0:LOC], p_t[0][:, 0:LOC], ACT.Copy).then_inc(pt_win, 1)

            @block.vector
            def _(dve):
                dve.wait_ge(const_in, 48)
                with dve.Fori(0, HP) as hp:
                    c = Counter(dve, chain, hp * 12)
                    for g in range(4):
                        half = slice((g % 2) * 512, (g % 2 + 1) * 512)
                        dve.wait_ge(proj_moved, START + hp * 5 + g + 1)
                        dve.wait_ge(roped, START + hp * 4 + g)
                        c.step(dve.tensor_tensor(cpart[:], plain[g][:], rope[:, 0, half], ALU.mult))
                        dve.wait_ge(rotated, hp * 4 + g + 1)
                        c.step(dve.tensor_tensor(spart[:], p_t[g % 2][:], rope[:, 1, half], ALU.mult))
                        if g == 0:
                            dve.wait_ge(padded, START + hp * 8)
                        if g == 2:
                            dve.wait_ge(scored, START + hp * PAIR)
                        dst = turned[g][:] if g < 2 else kwin[:, half]
                        dve.tensor_tensor(dst, cpart[:], spart[:], ALU.add).then_inc(roped, 1)
                    for n in range(PAIR + 2):
                        h, i, b = n // NT, n % NT, n % 2
                        if n < PAIR:
                            dve.wait_ge(scored, START + hp * PAIR + n + 1)
                            if i == 0:
                                dve.wait_ge(masked[h], hp + 1)
                            dve.wait_ge(exped, START + hp * PAIR + max(n - 1, 0))
                            dve.tensor_reduce(cmax[:, n:n + 1], p_ctx[b][:, 0:L], AX.X, ALU.max).then_inc(cmaxed, 1)
                            dve.tensor_tensor_reduce(biased[b][:], p_win[b][:, 0:LOC], table[h][:, i, :], 1.0, LOWEST,
                                                     ALU.add, ALU.max, rmax[:, n:n + 1]).then_inc(biased_ok[h], 1)
                            dve.wait_ge(cmaxed, hp * PAIR + n + 1)
                            dve.wait_ge(biased_ok[h], START + hp * NT + i + 1)
                            dve.tensor_scalar(nmax[:, n:n + 1], rmax[:, n:n + 1], cmax[:, n:n + 1], -1.0, ALU.max, ALU.mult).then_inc(maxed, 1)
                        if 1 <= n <= PAIR:
                            dve.wait_ge(probs_t, START + hp * PAIR + n)
                            dve.wait_ge(weighted, START + hp * PAIR + max(n - 2, 0))
                            dve.tensor_copy(probt[1 - b][:, LOC:KEYS], p_t[1][:, 0:L]).then_inc(pt_ctx, 1)
                        if n in (NT + 1, PAIR + 1):
                            h = n // NT - 1
                            cols = slice(NT * h, NT * h + NT)
                            dve.wait_ge(exped, START + hp * PAIR + NT * (h + 1))
                            c.step(dve.tensor_tensor(rsum[:, cols], psum1[:, cols], psum2[:, cols], ALU.add))
                            c.step(dve.reciprocal(rsum[:, cols], rsum[:, cols]))
                            dve.wait_ge(weighted, START + hp * PAIR + NT * (h + 1))
                            dst = s.na[:, :, bass.ds((hp * 2 + h) * HD, HD)]
                            dve.tensor_tensor(dst, p_o[:].rearrange("p (i d) -> p i d", i=NT),
                                              rsum[:, cols].unsqueeze(2).to_broadcast([P, NT, HD]), ALU.mult).then_inc(normed, 1)
                    assert c.n == 12, c.n

            @block.tensor
            def _(pe):
                pe.wait_ge(zeroed, 4)
                with pe.Fori(0, HP) as hp:
                    def project(g):
                        dst = (p_j, p_o)[g % 2]
                        if g == 0:
                            pe.wait_ge(w_in, (hp + 1) * 32)
                            pe.wait_ge(proj_moved, START + hp * 5)
                        elif g == 1:
                            pe.wait_ge(normed, START + hp * 2)
                        else:
                            pe.wait_ge(proj_moved, START + hp * 5 + g - 1)
                        cols = slice((g % 2) * 512, (g % 2 + 1) * 512) if g < 4 else slice(N, N + L)
                        for k in range(KD):
                            last = pe.matmul(dst[:, 0:cols.stop - cols.start], wqk[:, k, 0 if g < 2 else 1, :], s.ht[:, k, cols],
                                             start=(k == 0), stop=(k == KD - 1))
                        last.then_inc(projected, 1)

                    def rotate(g):
                        pe.wait_ge(proj_moved, START + hp * 5 + g + 1)
                        if g == 0:
                            pe.wait_ge(const_in, 48)
                            pe.wait_ge(pt_win, START + hp * PAIR)
                        elif g == 1:
                            pe.wait_ge(pt_ctx, START + hp * PAIR)
                        else:
                            pe.wait_ge(roped, START + hp * 4 + g - 1)
                        pe.matmul(p_t[g % 2][:], rot[:], plain[g][:], start=True, stop=True).then_inc(rotated, 1)

                    def score(n):
                        h, i, b = n // NT, n % NT, n % 2
                        pe.wait_ge(exped, START + hp * PAIR + max(n - 1, 0))
                        q = slice(i * P, (i + 1) * P)
                        keys = kwin.rearrange("p (r c) -> p r c", c=GW)[:, 4 * (i // 4):4 * (i // 4) + KR, COL0[i % 4]:COL0[i % 4] + KC]
                        pe.matmul(p_win[b][:, 0:LOC], qwin[h][:, q], keys, start=True, stop=True)
                        pe.matmul(p_ctx[b][:, 0:L], qctx[h][:, q], kctx[:], start=True, stop=True).then_inc(scored, 1)

                    def turn(n):
                        b = n % 2
                        pe.wait_ge(exped, START + hp * PAIR + n + 1)
                        pe.wait_ge(pt_win, START + hp * PAIR + n)
                        pe.wait_ge(pt_ctx, START + hp * PAIR + n)
                        for k in range(KEYS // P):
                            dst = p_t[0][:, k * P:(k + 1) * P] if k < 3 else p_t[1][:, (k - 3) * P:(k - 2) * P]
                            last = pe.transpose(dst, prob[b][:, k * P:(k + 1) * P], s.ident[:])
                        last.then_inc(probs_t, 1)

                    def weigh(n):
                        h, i, b = n // NT, n % NT, n % 2
                        pe.wait_ge(pt_win, START + hp * PAIR + n + 1)
                        pe.wait_ge(pt_ctx, START + hp * PAIR + n + 1)
                        if n == 0:
                            pe.wait_ge(v_in, (hp + 1) * 256)
                        if i == 0:
                            pe.wait_ge(normed, START + hp * 2 + h)
                        for k in range(KEYS // P):
                            if k < 3:
                                v = vh[:, 4 * (i % 4) + i // 4 + k, h * HD:(h + 1) * HD]
                            else:
                                v = vc[k - 3][:, h * HD:(h + 1) * HD]
                            last = pe.matmul(p_o[:, i * HD:(i + 1) * HD], probt[b][:, k * P:(k + 1) * P], v,
                                             start=(k == 0), stop=(k == KEYS // P - 1))
                        last.then_inc(weighted, 1)

                    vc = [s.vctx[:, k, bass.ds(hp * P, P)] for k in range(2)]
                    project(0)
                    project(1)
                    rotate(0)
                    project(2)
                    rotate(1)
                    project(3)
                    rotate(2)
                    project(4)
                    rotate(3)
                    pe.wait_ge(padded, START + (hp + 1) * 8)
                    pe.wait_ge(roped, START + (hp + 1) * 4)
                    pe.wait_ge(proj_moved, START + (hp + 1) * 5)
                    for n in range(PAIR + 2):
                        if n < PAIR:
                            score(n)
                        if 1 <= n <= PAIR:
                            turn(n - 1)
                        if n >= 2:
                            weigh(n - 2)


def mix_and_route(nc, m, a, s):
    with ExitStack() as stack:
        t = Mem(nc, stack)
        wo = t.sb("wo", [P, KD, D])
        free = s.ht[:].rearrange("p k n -> p (k n)")
        xrow = free[:, 0:4 * D].rearrange("p (i n) -> p i n", i=4)
        yt = free[:, 4 * D:8 * D].rearrange("p (k n) -> p k n", k=KD)
        xp = free[:, 8 * D:10 * D].rearrange("p (b n) -> p b n", b=2)
        wr = t.sb("wr", [P, KD, NG + NE])
        before = t.sb("before", [P, P])
        desc, base, blk, ids = t.sb("desc", [P, NT, EPG]), t.sb("base", [P, NE]), t.sb("blk", [1, OVB, NE]), t.sb("ids", [P, 2, NT, 4], I32)
        junk = t.sb("junk4", [P, D])
        epsb = t.sb("epsb4", [P, 1])
        ss = t.sb("ss4", [P, 3, NT])
        root, rstd, tmp = t.sb("root4", [P, 3, NT]), t.sb("rstd4", [P, 3, NT]), t.sb("tmp4", [P, 3, NT])
        empty = t.sb("empty", [P, SLOTS * 4 // P], I32)
        lg = t.sb("lg", [P, NT, NG + NE])
        p_y = [t.ps(f"p_y{b}", [P, 2, 512]) for b in range(2)]
        p_t = [t.ps(f"p_t4{b}", [P, 512]) for b in range(2)]
        p_l, p_r = t.ps("p_l", [P, 512]), t.ps("p_r", [P, 2, NE * NT])

        w_in, c_in, xp_in = t.sem("wo_in"), t.sem("c4_in"), [t.sem(f"xp_in{b}") for b in range(2)]
        pool_ok, squared, rooted, scaled = t.sem("pool_ok4"), t.sem("squared4"), t.sem("rooted4"), t.sem("scaled4")
        turned, t_act, t_dve = t.sem("turned4"), t.sem("t_act4"), t.sem("t_dve4")
        mixed, added, squared2, rooted2, scaled2 = t.sem("mixed"), t.sem("added"), t.sem("squared5"), t.sem("rooted5"), t.sem("scaled5")
        logits, logits_moved, h_out = t.sem("logits"), t.sem("logits_moved"), t.sem("h_out")
        chosen, ranked, slots_ok, exps_in, exps = t.sem("chosen"), t.sem("ranked"), t.sem("slots_ok"), t.sem("exps_in"), t.sem("exps")
        table_empty, scattered, chain = t.sem("table_empty"), t.sem("scattered"), t.sem("chain4")
        small = lambda name, *shape: t.sb(name, [P, *shape])
        gmax, goh, gsum, gdif = small("gmax", NT), small("goh", NT, NG), small("gsum", NT), small("gdif", NT, NG)
        lsel, lpart, lmax = small("lsel", NT, EPG), small("lpart", NT, NG, EPG), small("lmax", 2, NT)
        eoh, key, kmax = small("eoh", 2, NT, EPG), small("key", NT, EPG), small("kmax", NT)
        wexp, gates, den = small("wexp", NT), small("gates", 2, NT), small("den", NT)
        one_e, both = small("one_e", 2, NT, NE), small("both", NT, NE)
        offs, rank, count = small("offs", NT + 1, NE), small("rank", NT, NE), small("count", NT, NE)
        over, upto, ovb = small("over", NE), small("upto", NE), small("ovb", NE)
        pick, rk, bs, ob = small("pick", NT, NE), small("rk", 2, NT), small("bs", 2, NT), small("ob", 2, NT)
        slot = t.sb("slot", [P, 2, NT], I32)
        cmpb, cntb = t.sb("cmpb", [1, OVB, NE]), t.sb("cntb", [1, OVB + 1])

        with nc.Block() as block:

            @block.sync
            def _(sp):
                for dst, src in ((before, a.before), (desc, a.desc), (base, a.base), (blk, a.blk), (ids, a.ids)):
                    sp.dma_start(dst[:], src).then_inc(c_in, 16)
                sp.dma_start(wr[:], a.w_router.rearrange("(k p) n -> p k n", p=P)).then_inc(c_in, 16)
                sp.dma_start(wo[:], a.w_out.rearrange("(k p) n -> p k n", p=P)).then_inc(w_in, 16)
                for i in range(NT):
                    if i >= 2:
                        sp.wait_ge(added, 2 * (i - 1))
                    sp.dma_start(xp[:, i % 2, :], a.x_perm[i * P:(i + 1) * P, :]).then_inc(xp_in[i % 2], 16)
                for j in range(RING):
                    load_chunk(sp, a, s.raw, s.loaded, 0, j, j)

            @block.gpsimd
            def _(pool):
                pool.memset(epsb[:], EPS).then_inc(pool_ok, 1)
                pool.memset(offs[:, 0, :], 0.0).then_inc(pool_ok, 1)
                pool.memset(over[:], 0.0).then_inc(pool_ok, 1)
                pool.memset(empty[:], SKIP).then_inc(pool_ok, 1)
                pool.wait_ge(pool_ok, 4)
                pool.dma_start(a.slot_rows.rearrange("(p n) c -> p (n c)", p=P), empty[:]).then_inc(table_empty, 16)
                pool.wait_ge(table_empty, 16)
                pool.wait_ge(slots_ok, 3)
                for k in range(2):
                    for i in range(NT):
                        pool.indirect_dma_start(a.slot_rows, bass.IndirectOffsetOnAxis(ap=slot[:, k, i:i + 1], axis=0),
                                                ids[:, k, i, :], None, bounds_check=SLOTS - 1).then_inc(scattered, 16)
                pool.wait_ge(scattered, 16 * 2 * NT)

            def norm_groups(act):
                for g in range(2):
                    for i in range(4 * g, 4 * g + 4):
                        for w, (src, width) in enumerate(((s.fout[:, i, :], DF), (s.na[:, i, :], DN))):
                            act.wait_ge(squared, 2 * i + w)
                            act.activation(junk[:, 0:width], src, ACT.Square, scale=width ** -0.5, accum_out=ss[:, w, i:i + 1]).then_inc(squared, 1)
                    act.wait_ge(squared, 8 * (g + 1))
                    act.wait_ge(pool_ok, 4)
                    four = slice(4 * g, 4 * g + 4)
                    act.activation(root[:, 0:2, four], ss[:, 0:2, four], ACT.Sqrt, bias=epsb[:, 0:1]).then_inc(rooted, 1)

            @block.scalar
            def _(act):
                norm_groups(act)

                def move_y(g):
                    for k in range(0, KD, 2):
                        act.wait_ge(turned, 8 * g + k + 1)
                        if g == 1 and k == 0:
                            act.wait_ge(mixed, 4)
                        act.activation(yt[:, k, :], p_t[k % 2][:], ACT.Copy, scale=s.vcol[:, 80 + k:81 + k]).then_inc(t_act, 1)

                def norm_x(g):
                    for i in range(4 * g, 4 * g + 4):
                        act.wait_ge(added, 2 * (i + 1))
                        act.wait_ge(squared2, i)
                        act.activation(junk[:], s.x1[:, i, :], ACT.Square, accum_out=ss[:, 2, i:i + 1]).then_inc(squared2, 1)
                    act.wait_ge(squared2, 4 * g + 4)
                    act.activation(root[:, 2, 4 * g:4 * g + 4], ss[:, 2, 4 * g:4 * g + 4], ACT.Sqrt, scale=1.0 / D,
                                   bias=epsb[:, 0:1]).then_inc(rooted2, 1)

                def store_x(g):
                    for i in range(4):
                        act.wait_ge(scaled2, 4 * g + i + 1)
                        n = 4 * g + i
                        act.dma_start(a.h_rows[n * P:(n + 1) * P, :], xrow[:, i, :]).then_inc(h_out, 16)

                def move_x(g):
                    for k in range(0, KD, 2):
                        act.wait_ge(turned, 16 + 8 * g + k + 1)
                        act.wait_ge(mixed, NT)
                        if g == 1:
                            act.wait_ge(logits, 1)
                        act.activation(yt[:, k, :], p_t[k % 2][:], ACT.Identity, scale=s.scale2[:, k:k + 1],
                                       bias=s.shift2[:, k:k + 1]).then_inc(t_act, 1)
                move_y(0)
                move_y(1)
                norm_x(0)
                store_x(0)
                norm_x(1)
                move_x(0)
                store_x(1)
                move_x(1)
                act.wait_ge(exps_in, 1)
                act.activation(gdif[:], gdif[:], ACT.Exp).then_inc(exps, 1)
                act.wait_ge(exps_in, 2)
                act.activation(wexp[:], wexp[:], ACT.Exp).then_inc(exps, 1)
                act.wait_ge(h_out, 16 * NT)

            @block.vector
            def _(dve):
                c = Counter(dve, chain)
                step = c.step
                tt, ts, stt = dve.tensor_tensor, dve.tensor_scalar, dve.scalar_tensor_tensor

                def norm_groups(g):
                    four = slice(4 * g, 4 * g + 4)
                    dve.wait_ge(rooted, g + 1)
                    step(dve.reciprocal(rstd[:, 0:2, four], root[:, 0:2, four]))
                    newton(dve, c, rstd[:, 0:2, four], ss[:, 0:2, four], tmp[:, 0:2, four], 1, n=4)
                    for n in range(4 * g, 4 * g + 4):
                        ts(s.fout[:, n, :], s.fout[:, n, :], rstd[:, 0, n:n + 1], None, ALU.mult).then_inc(scaled, 1)
                        ts(s.na[:, n, :], s.na[:, n, :], rstd[:, 1, n:n + 1], None, ALU.mult).then_inc(scaled, 1)

                def move_y(g):
                    for k in range(1, KD, 2):
                        dve.wait_ge(turned, 8 * g + k + 1)
                        if g == 1 and k == 1:
                            dve.wait_ge(mixed, 4)
                        ts(yt[:, k, :], p_t[k % 2][:], s.vcol[:, 80 + k:81 + k], None, ALU.mult).then_inc(t_dve, 1)

                def residual(g):
                    for n in range(4 * g, 4 * g + 4):
                        dve.wait_ge(mixed, n + 1)
                        dve.wait_ge(xp_in[n % 2], 16 * (n // 2 + 1))
                        x1 = s.x1[:, n, :]
                        dve.tensor_tensor(x1.rearrange("p (c n) -> p c n", c=2), p_y[n % 2][:],
                                          s.gate1[:].rearrange("p (c n) -> p c n", c=2), ALU.mult).then_inc(added, 1)
                        dve.wait_ge(added, 2 * n + 1)
                        dve.tensor_tensor(x1, x1, xp[:, n % 2, :], ALU.add).then_inc(added, 1)

                def norm_x(g):
                    dve.wait_ge(rooted2, g + 1)
                    four = slice(4 * g, 4 * g + 4)
                    step(dve.reciprocal(rstd[:, 2, four], root[:, 2, four]))
                    newton(dve, c, rstd[:, 2, four], ss[:, 2, four], tmp[:, 2, four], D, n=4)
                    if g == 1:
                        dve.wait_ge(h_out, 64)
                        dve.wait_ge(turned, 24)
                    for i in range(4):
                        n = 4 * g + i
                        ts(xrow[:, i, :], s.x1[:, n, :], rstd[:, 2, n:n + 1], None, ALU.mult).then_inc(scaled2, 1)

                def move_x(g):
                    for k in range(1, KD, 2):
                        dve.wait_ge(turned, 16 + 8 * g + k + 1)
                        dve.wait_ge(mixed, NT)
                        if g == 1:
                            dve.wait_ge(logits, 1)
                        ts(yt[:, k, :], p_t[k % 2][:], s.scale2[:, k:k + 1], s.shift2[:, k:k + 1], ALU.mult, ALU.add).then_inc(t_dve, 1)

                def take_logits(g):
                    dve.wait_ge(logits, g + 1)
                    step(dve.tensor_copy(lg[:, 4 * g:4 * g + 4, :], p_l[:, 0:4 * (NG + NE)].rearrange("p (i n) -> p i n", i=4)))
                    dve.sem_inc(logits_moved, 1)

                norm_groups(0)
                move_y(0)
                norm_groups(1)
                dve.wait_ge(c_in, 96)
                residual(0)
                move_y(1)
                norm_x(0)
                residual(1)
                move_x(0)
                norm_x(1)
                take_logits(0)
                move_x(1)
                take_logits(1)

                def bc(x, n):
                    return x.unsqueeze(2).to_broadcast([P, NT, n])

                def first_match(dst, values, top, d):
                    n = values.shape[2]
                    step(tt(key[:, :, 0:n], values, bc(top, n), ALU.is_equal))
                    step(tt(key[:, :, 0:n], key[:, :, 0:n], d, ALU.mult))
                    step(dve.tensor_reduce(kmax[:], key[:, :, 0:n], AX.X, ALU.max))
                    step(tt(dst, key[:, :, 0:n], bc(kmax[:], n), ALU.is_equal))

                lgg, lge = lg[:, :, 0:NG], lg[:, :, NG:NG + NE].rearrange("p i (g e) -> p i g e", g=NG)
                step(dve.tensor_reduce(gmax[:], lgg, AX.X, ALU.max))
                step(tt(gdif[:], lgg, bc(gmax[:], NG), ALU.subtract))
                dve.sem_inc(exps_in, 1)
                first_match(goh[:], lgg, gmax[:], desc[:, :, EPG - NG:EPG])
                step(tt(lpart[:], lge, goh[:].unsqueeze(3).to_broadcast([P, NT, NG, EPG]), ALU.mult))
                step(tt(lsel[:], lpart[:, :, 0, :], lpart[:, :, 1, :], ALU.add))
                step(tt(lsel[:], lsel[:], lpart[:, :, 2, :], ALU.add))
                step(tt(lsel[:], lsel[:], lpart[:, :, 3, :], ALU.add))
                step(dve.tensor_reduce(lmax[:, 0, :], lsel[:], AX.X, ALU.max))
                first_match(eoh[:, 0], lsel[:], lmax[:, 0, :], desc[:])
                step(stt(lsel[:], eoh[:, 0], NEG, lsel[:], ALU.mult, ALU.add))
                step(dve.tensor_reduce(lmax[:, 1, :], lsel[:], AX.X, ALU.max))
                first_match(eoh[:, 1], lsel[:], lmax[:, 1, :], desc[:])
                step(tt(wexp[:], lmax[:, 1, :], lmax[:, 0, :], ALU.subtract))
                dve.sem_inc(exps_in, 1)
                for k in range(2):
                    step(tt(one_e[:, k].rearrange("p i (g e) -> p i g e", g=NG), goh[:].unsqueeze(3).to_broadcast([P, NT, NG, EPG]),
                            eoh[:, k].unsqueeze(2).to_broadcast([P, NT, NG, EPG]), ALU.mult))
                step(tt(both[:], one_e[:, 0], one_e[:, 1], ALU.add))
                dve.sem_inc(chosen, 1)
                dve.wait_ge(exps, 1)
                step(dve.tensor_reduce(gsum[:], gdif[:], AX.X, ALU.add))
                dve.wait_ge(exps, 2)
                step(ts(den[:], wexp[:], 1.0, None, ALU.add))
                step(tt(den[:], den[:], gsum[:], ALU.mult))
                step(dve.reciprocal(gates[:, 0, :], den[:]))
                step(tt(gates[:, 1, :], gates[:, 0, :], wexp[:], ALU.mult))
                for k in range(2):
                    dve.tensor_copy(ids[:, k, :, 2].bitcast(F32), gates[:, k, :]).then_inc(slots_ok, 1)
                dve.wait_ge(ranked, 1)
                step(dve.tensor_copy(count[:], p_r[:, 1, :].rearrange("p (i e) -> p i e", e=NE)))
                for i in range(NT):
                    step(tt(offs[:, i + 1, :], offs[:, i, :], count[:, i, :], ALU.add))
                step(tt(rank[:], p_r[:, 0, :].rearrange("p (i e) -> p i e", e=NE), offs[:, 0:NT, :], ALU.add))
                for i in range(1, N // CAP):
                    step(stt(over[:], offs[:, NT, :], float(CAP * i), over[:], ALU.is_gt, ALU.add))
                step(dve.tensor_tensor_scan(upto[:], s.ones[:, 0:NE], over[:], 0.0, ALU.mult, ALU.add))
                step(tt(ovb[:], upto[:], over[:], ALU.subtract))
                step(ts(ovb[:], ovb[:], float(CAP), float((NE - 1) * CAP), ALU.mult, ALU.add))
                for k in range(2):
                    for dst, src in ((rk, rank[:]), (bs, base[:].unsqueeze(1).to_broadcast([P, NT, NE])), (ob, ovb[:].unsqueeze(1).to_broadcast([P, NT, NE]))):
                        step(tt(pick[:], one_e[:, k], src, ALU.mult))
                        step(dve.tensor_reduce(dst[:, k, :], pick[:], AX.X, ALU.add))
                step(tt(ob[:], ob[:], bs[:], ALU.subtract))
                step(tt(bs[:], bs[:], rk[:], ALU.add))
                step(ts(rk[:], rk[:], float(CAP), None, ALU.is_ge))
                step(tt(rk[:], rk[:], ob[:], ALU.mult))
                step(tt(rk[:], rk[:], bs[:], ALU.add))
                dve.tensor_copy(slot[:], rk[:]).then_inc(slots_ok, 1)
                step(tt(cmpb[:], upto[0:1, :].unsqueeze(1).to_broadcast([1, OVB, NE]), blk[:], ALU.is_le))
                step(dve.tensor_reduce(cntb[:, 0:OVB], cmpb[:], AX.X, ALU.add))
                step(ts(cntb[:, 0:OVB], cntb[:, 0:OVB], float(NE - 1), None, ALU.min))
                step(dve.tensor_copy(cntb[:, OVB:OVB + 1], upto[0:1, NE - 1:NE]))
                step(dve.tensor_copy(s.blocks[:], cntb[:]))

            @block.tensor
            def _(pe):
                def turn(run):
                    g = run % 2
                    for k in range(KD):
                        u = 8 * run + k
                        if u >= 2:
                            pe.wait_ge(t_act if k % 2 == 0 else t_dve, (u - 2) // 2 + 1)
                        for i in range(4):
                            n = 4 * g + i
                            if run >= 2:
                                src = xrow[:, i, k * P:(k + 1) * P]
                            elif k < 2:
                                src = s.fout[:, n, k * P:(k + 1) * P]
                            else:
                                src = s.na[:, n, (k - 2) * P:(k - 1) * P]
                            last = pe.transpose(p_t[k % 2][:, i * P:(i + 1) * P], src, s.ident[:])
                        last.then_inc(turned, 1)
                    pe.wait_ge(t_act, 4 * (run + 1))
                    pe.wait_ge(t_dve, 4 * (run + 1))

                def mix(g):
                    for i in range(4):
                        n = 4 * g + i
                        if n >= 2:
                            pe.wait_ge(added, 2 * (n - 2) + 1)
                        for h in range(2):
                            for k in range(KD):
                                last = pe.matmul(p_y[n % 2][:, h, :], yt[:, k, i * P:(i + 1) * P], wo[:, k, h * 512:(h + 1) * 512],
                                                 start=(k == 0), stop=(k == KD - 1))
                        last.then_inc(mixed, 1)

                def route(g):
                    if g == 1:
                        pe.wait_ge(logits_moved, 1)
                    for i in range(4):
                        for k in range(KD):
                            last = pe.matmul(p_l[:, i * 36:(i + 1) * 36], yt[:, k, i * P:(i + 1) * P], wr[:, k, :],
                                             start=(k == 0), stop=(k == KD - 1))
                    last.then_inc(logits, 1)

                pe.wait_ge(c_in, 96)
                pe.wait_ge(w_in, 16)
                for g in range(2):
                    pe.wait_ge(scaled, 8 * (g + 1))
                    turn(g)
                    mix(g)
                for g in range(2):
                    pe.wait_ge(scaled2, 4 * (g + 1))
                    turn(2 + g)
                    route(g)
                pe.wait_ge(chosen, 1)
                flat = both[:].rearrange("p i e -> p (i e)")
                pe.matmul(p_r[:, 0, :], before[:], flat, start=True, stop=True)
                pe.matmul(p_r[:, 1, :], s.ones[:], flat, start=True, stop=True).then_inc(ranked, 1)


class ExpertSteps:

    def __init__(self, t, a, s, buf):
        self.a, self.s, self.buf, self.loaded = a, s, buf, s.loaded
        self.high_ok = [t.sem(f"high_ok{j}") for j in range(CHUNKS)]
        self.low_ok = [t.sem(f"low_ok{j}") for j in range(CHUNKS)]
        self.used = [t.sem(f"used{j}") for j in range(CHUNKS)]
        self.gathered = [t.sem(f"gathered{b}") for b in range(2)]
        self.scattered = [t.sem(f"scattered{b}") for b in range(2)]
        self.x_turned, self.x_act, self.x_dve = t.sem("turned_5"), t.sem("act_5"), t.sem("dve_5")
        self.x_high, self.x_low = t.sem("high_5"), t.sem("low_5")
        self.silu_ok, self.h_ok, self.h_turned = t.sem("silu_ok_5"), t.sem("h_ok_5"), t.sem("h_turned_5")
        self.h_high, self.h_low = t.sem("h_high_5"), t.sem("h_low_5")
        self.y_ok, self.y_free = t.sem("y_ok_5"), t.sem("y_free_5")
        self.token_ok, self.row_ok = t.sem("token_ok_5"), t.sem("row_ok_5")
        self.passed = t.sem("passed5")

    def prime(self, pool):
        for sem in (*self.used, *self.low_ok, self.h_ok, self.y_ok):
            pool.sem_inc(sem, START)
        pool.sem_inc(self.y_free, START + 1)

    def load(self, sp, e, j, ring):
        load_chunk(sp, self.a, self.buf.raw, self.loaded, e, j, ring)

    def high(self, act, n, j, ring, loads):
        act.wait_ge(self.loaded[ring], 16 * loads)
        act.wait_ge(self.used[j], START + n)
        act.activation(self.buf.high[j][:], self.buf.raw[ring][:], ACT.Copy).then_inc(self.high_ok[j], 1)

    def low(self, eng, n, j, ring):
        on_pool = eng is self.s.pool
        if on_pool != (j in POOL_LOWS):
            return
        eng.wait_ge(self.high_ok[j], n + 1)
        if on_pool:
            eng.sem_inc(self.passed, 1)
        eng.tensor_tensor(self.buf.low[j][:], self.buf.raw[ring][:], self.buf.high[j][:], ALU.subtract).then_inc(self.low_ok[j], 1)

    def pick(self, pool, n, dst, column, ok):
        pool.tensor_copy(dst[:], self.slots(n, column)).then_inc(ok, 1)
        pool.wait_ge(ok, n + 1)
        pool.sem_inc(self.passed, 1)

    def gather(self, pool, n, b):
        self.pick(pool, n, self.buf.tokens[b], 0, self.token_ok)
        pool.indirect_dma_start(self.buf.xg[b][:], None, self.a.h_rows, bass.IndirectOffsetOnAxis(ap=self.buf.tokens[b][:], axis=0),
                                bounds_check=N - 1, oob_is_err=False).then_inc(self.gathered[b], 16)

    def scatter(self, pool, n, b):
        pool.wait_ge(self.y_ok, START + n + 1)
        pool.sem_inc(self.passed, 1)
        self.pick(pool, n, self.buf.rows[b], 1, self.row_ok)
        pool.indirect_dma_start(self.a.y_rows, bass.IndirectOffsetOnAxis(ap=self.buf.rows[b][:], axis=0), self.buf.y[b][:], None,
                                bounds_check=2 * N - 1, oob_is_err=False).then_inc(self.scattered[b], 16)

    def release_y(self, pool, b, times):
        pool.wait_ge(self.scattered[b], 16 * times)
        pool.sem_inc(self.y_free, 1)

    def slots(self, n, column):
        return self.buf.sid[:, bass.ds(n, 1), column:column + 1].rearrange("p b c -> p (b c)")

    def turn_x(self, pe, n, b, times):
        pe.wait_ge(self.gathered[b], 16 * times)
        for k in range(KD):
            last = pe.transpose(self.buf.p_x[k // 4][:, k % 4, :], self.buf.xg[b][:, k * P:(k + 1) * P], self.s.ident[:])
        last.then_inc(self.x_turned, 1)

    def move_x(self, eng, n):
        eng.wait_ge(self.x_turned, n + 1)
        on_act = eng is self.s.act
        buf = self.buf
        for k in range(0, 4) if on_act else range(4, 8):
            dst, src = buf.xf[:, k, :], buf.p_x[k // 4][:, k % 4, :]
            sc, sh = self.s.scale2[:, k:k + 1], self.s.shift2[:, k:k + 1]
            if on_act:
                last = eng.activation(dst, src, ACT.Identity, scale=sc, bias=sh)
            else:
                last = eng.tensor_scalar(dst, src, sc, sh, ALU.mult, ALU.add)
        last.then_inc(self.x_act if on_act else self.x_dve, 1)
        if on_act:
            eng.wait_ge(self.x_act, n + 1)
            eng.wait_ge(self.x_dve, n + 1)
            eng.activation(buf.x_high[:], buf.xf[:], ACT.Copy).then_inc(self.x_high, 1)
        else:
            eng.wait_ge(self.x_high, n + 1)
            eng.tensor_tensor(buf.x_low[:], buf.xf[:], buf.x_high[:], ALU.subtract).then_inc(self.x_low, 1)

    def products(self, pe, dst, high, low, w_high, w_low, start, stop):
        pe.matmul(dst, high, w_high, start=start, stop=False)
        pe.matmul(dst, high, w_low, start=False, stop=False)
        return pe.matmul(dst, low, w_high, start=False, stop=stop)

    def gate_up(self, pe, n):
        buf = self.buf
        pe.wait_ge(self.x_low, n + 1)
        pe.wait_ge(self.h_ok, START + n)
        for j in range(4):
            pe.wait_ge(self.low_ok[j], START + n + 1)
            dst = (buf.p_g, buf.p_u)[j // 2]
            for i in range(4):
                k = 4 * (j % 2) + i
                w = slice(i * DE, (i + 1) * DE)
                last = self.products(pe, dst[:], buf.x_high[:, k, :], buf.x_low[:, k, :], buf.high[j][:, w], buf.low[j][:, w],
                                     start=(k == 0), stop=(k == KD - 1))
            last.then_inc(self.used[j], 1)

    def silu(self, act, n):
        act.wait_ge(self.used[3], START + n + 1)
        act.activation(self.buf.silu[:], self.buf.p_g[:], ACT.Silu).then_inc(self.silu_ok, 1)

    def multiply(self, dve, n):
        dve.wait_ge(self.silu_ok, n + 1)
        dve.tensor_tensor(self.buf.h[:], self.buf.silu[:], self.buf.p_u[:], ALU.mult).then_inc(self.h_ok, 1)

    def turn_h(self, pe, n):
        pe.wait_ge(self.h_ok, START + n + 1)
        for k in range(KE):
            last = pe.transpose(self.buf.p_h[:, k, :], self.buf.h[:, k * P:(k + 1) * P], self.s.ident[:])
        last.then_inc(self.h_turned, 1)

    def high_h(self, act, n):
        act.wait_ge(self.h_turned, n + 1)
        act.activation(self.buf.h_high[:], self.buf.p_h[:], ACT.Copy).then_inc(self.h_high, 1)

    def low_h(self, dve, n):
        dve.wait_ge(self.h_high, n + 1)
        dve.tensor_tensor(self.buf.h_low[:], self.buf.p_h[:], self.buf.h_high[:], ALU.subtract).then_inc(self.h_low, 1)

    def down(self, pe, n):
        buf = self.buf
        pe.wait_ge(self.h_low, n + 1)
        pe.wait_ge(self.y_ok, START + n)
        for j in (4, 5):
            pe.wait_ge(self.low_ok[j], START + n + 1)
            for h in range(2):
                for i in range(2):
                    k = 2 * (j - 4) + i
                    w = slice(i * D + h * 512, i * D + (h + 1) * 512)
                    last = self.products(pe, buf.p_y[:, h, :], buf.h_high[:, k, :], buf.h_low[:, k, :], buf.high[j][:, w], buf.low[j][:, w],
                                         start=(k == 0), stop=(k == KE - 1))
            last.then_inc(self.used[j], 1)

    def move_y(self, dve, n, b):
        dve.wait_ge(self.used[5], START + n + 1)
        dve.wait_ge(self.y_free, START + n)
        dve.scalar_tensor_tensor(self.buf.y[b][:].rearrange("p (c n) -> p c n", c=2), self.buf.p_y[:], self.slots(n, 2).bitcast(F32),
                                 self.s.gate2[:].rearrange("p (c n) -> p c n", c=2), ALU.mult, ALU.mult).then_inc(self.y_ok, 1)


def load_chunk(sp, a, raw, loaded, e, j, ring):
    if j < 4:
        src = (a.w_gate, a.w_up)[j // 2][e][512 * (j % 2):512 * (j % 2 + 1), :]
    else:
        src = a.w_down[e][256 * (j - 4):256 * (j - 3), :]
    src = src.rearrange("(k p) n -> p k n", p=P)
    k = src.shape[1]
    sp.dma_start(raw[ring][:].rearrange("p (k n) -> p k n", k=k), src).then_inc(loaded[ring], 16)


class Place:

    def __init__(self, n0, it, chunk):
        number = 6 * n0 + chunk
        self.ring = number % RING
        self.loads = it * (12 // RING) + number // RING + 1 - (1 if self.ring < 2 and n0 > 0 else 0)


def experts(nc, a, s):
    with ExitStack() as stack:
        t = Mem(nc, stack)
        x = buf = Buffers()
        x.raw = s.raw
        high = [t.sb(f"w_high{j}", [P, CHUNK], F32R) for j in range(CHUNKS)]
        low = [t.sb(f"w_low{j}", [P, CHUNK], F32R) for j in range(CHUNKS)]
        sid = t.sb("sid", [CAP, NE + OVB, 4], I32)
        xg = [t.sb(f"xg{b}", [CAP, D]) for b in range(2)]
        tokens, rows = ([t.sb(f"{name}{b}", [CAP, 1], I32) for b in range(2)] for name in ("tokens", "rows"))
        xf = t.sb("xf", [P, KD, CAP])
        x_high, x_low = t.sb("x_high", [P, KD, CAP], F32R), t.sb("x_low", [P, KD, CAP], F32R)
        y = [t.sb(f"y5{b}", [CAP, D]) for b in range(2)]
        silu, h = t.sb("silu", [CAP, DE]), t.sb("h5", [CAP, DE])
        h_high, h_low = t.sb("h_high", [P, KE, CAP], F32R), t.sb("h_low", [P, KE, CAP], F32R)
        p_x = [t.ps(f"p_x{b}", [P, 4, CAP]) for b in range(2)]
        p_g, p_u = t.ps("p_g", [CAP, DE]), t.ps("p_u", [CAP, DE])
        p_h, p_y = t.ps("p_h", [P, KE, CAP]), t.ps("p_y5", [CAP, 2, 512])
        x.high, x.low, x.sid, x.xg, x.xf, x.x_high, x.x_low, x.y = high, low, sid, xg, xf, x_high, x_low, y
        x.silu, x.h, x.h_high, x.h_low, x.p_x, x.p_g, x.p_u, x.p_h, x.p_y = silu, h, h_high, h_low, p_x, p_g, p_u, p_h, p_y
        x.tokens, x.rows = tokens, rows
        q = ExpertSteps(t, a, s, buf)
        first_sid_in, sid_in, xg_zero = t.sem("first_sid_in"), t.sem("sid_in"), t.sem("xg_zero")
        PAIRS = NE // 2 - 1
        LOADS = NE * CHUNKS // RING

        def run(engine, step):
            step(0, 0, 0)
            with engine.Fori(0, PAIRS) as it:
                for n0 in (1, 2):
                    step(it * 2 + n0, n0, it)
            step(NE - 1, 1, PAIRS)

        def first(n0):
            return n0 == 0

        def last(it):
            return it is PAIRS

        with nc.Block() as block:

            @block.sync
            def _(sp):
                table = a.slot_rows.rearrange("(b p) c -> p b c", p=CAP)
                sp.dma_start(sid[:, 0:2, :], table[:, 0:2, :]).then_inc(first_sid_in, 16)
                sp.dma_start(sid[:, 2:, :], table[:, 2:, :]).then_inc(sid_in, 16)

                def step(n, n0, it):
                    if first(n0):
                        return
                    for j in range(CHUNKS):
                        if j < 2:
                            sp.wait_ge(q.low_ok[j + 2], START + n)
                        elif j < 4:
                            sp.wait_ge(q.low_ok[j - 2], START + n)
                            sp.sem_inc(q.passed, 1)
                            sp.wait_ge(q.low_ok[j + 2], START + n - 1)
                        else:
                            sp.wait_ge(q.low_ok[j - 4], START + n + 1)
                        sp.sem_inc(q.passed, 1)
                        q.load(sp, n if j < 4 else n - 1, j, Place(n0, it, j).ring)

                run(sp, step)
                for j in (4, 5):
                    sp.wait_ge(q.low_ok[j - 2], START + NE)
                    q.load(sp, NE - 1, j, j - 4)

            @block.gpsimd
            def _(pool):
                q.prime(pool)
                for b in range(2):
                    pool.memset(xg[b][:], 0.0).then_inc(xg_zero, 1)
                pool.wait_ge(xg_zero, 2)
                pool.wait_ge(first_sid_in, 16)
                q.gather(pool, 0, 0)
                q.gather(pool, 1, 1)
                pool.wait_ge(sid_in, 16)
                for j in range(4):
                    q.low(pool, 0, j, Place(0, 0, j).ring)

                def step(n, b, more, scatters, old, splits=True):
                    if scatters:
                        for j in (4, 5):
                            q.low(pool, n - 1, j, Place(b, 0, j).ring)
                    if more:
                        pool.wait_ge(q.x_turned, n + 1)
                        pool.sem_inc(q.passed, 1)
                        q.gather(pool, n + 2, b)
                    if splits:
                        for j in range(4):
                            q.low(pool, n + 1, j, Place(b + 1, 0, j).ring)
                    if scatters:
                        q.scatter(pool, n - 1, 1 - b)
                    if old is not None:
                        q.release_y(pool, b, old)

                step(0, 0, True, False, None)
                step(1, 1, True, True, None)
                step(2, 0, True, True, 1)
                with pool.Fori(0, NE // 2 - 3) as it:
                    step(it * 2 + 3, 1, True, True, it + 1)
                    step(it * 2 + 4, 0, True, True, it + 2)
                for n in range(NE - 3, NE + 1):
                    step(n, n % 2, n < NE - 2, True, (n - 2) // 2 + 1, splits=n < NE - 1)
                q.release_y(pool, 1, NE // 2)

            @block.scalar
            def _(act):
                for j in range(4):
                    q.high(act, 0, j, Place(0, 0, j).ring, 1)
                q.move_x(act, 0)

                def step(n, n0, it):
                    if not first(n0):
                        for j in (4, 5):
                            p = Place(n0, it, j)
                            q.high(act, n - 1, j, p.ring, p.loads)
                    for j in range(4):
                        if j == 3:
                            q.silu(act, n)
                        if not last(it):
                            p = Place(n0 + 1, it, j)
                            q.high(act, n + 1, j, p.ring, p.loads)
                    if not last(it):
                        q.move_x(act, n + 1)
                    q.high_h(act, n)

                run(act, step)
                for j in (4, 5):
                    q.high(act, NE - 1, j, j - 4, LOADS)

            @block.vector
            def _(dve):
                for j in range(4):
                    q.low(dve, 0, j, Place(0, 0, j).ring)
                dve.wait_ge(first_sid_in, 16)
                dve.wait_ge(sid_in, 16)
                q.move_x(dve, 0)

                def step(n, n0, it):
                    if not first(n0):
                        for j in (4, 5):
                            q.low(dve, n - 1, j, Place(n0, it, j).ring)
                    for j in range(4):
                        if j == 3:
                            q.multiply(dve, n)
                        if not last(it):
                            q.low(dve, n + 1, j, Place(n0 + 1, it, j).ring)
                    if not last(it):
                        q.move_x(dve, n + 1)
                    if not first(n0):
                        q.move_y(dve, n - 1, 1 - n0 % 2)
                    q.low_h(dve, n)

                run(dve, step)
                for j in (4, 5):
                    q.low(dve, NE - 1, j, j - 4)
                q.move_y(dve, NE - 1, 1)

            @block.tensor
            def _(pe):
                q.turn_x(pe, 0, 0, 1)

                def step(n, n0, it):
                    q.gate_up(pe, n)
                    if not last(it):
                        q.turn_x(pe, n + 1, 1 - n0 % 2, it + (n0 + 1) // 2 + 1)
                    if not first(n0):
                        q.down(pe, n - 1)
                    q.turn_h(pe, n)

                run(pe, step)
                q.down(pe, NE - 1)

        def each(engine, body):
            count = engine.value_load(s.blocks[0:1, OVB:OVB + 1], min_val=0, max_val=OVB)
            with engine.If(count > 0):
                with engine.Fori(0, count) as n:
                    body(n, n + NE)

        with nc.Block() as block:

            @block.sync
            def _(sp):
                def body(n, block):
                    e = sp.value_load(s.blocks[0:1, bass.ds(n, 1)], min_val=0, max_val=NE - 1)
                    for j in range(CHUNKS):
                        if j >= RING:
                            sp.wait_ge(q.low_ok[j - RING], START + block + 1)
                            sp.sem_inc(q.passed, 1)
                        q.load(sp, e, j, j % RING)
                    sp.wait_ge(q.scattered[0], (n + NE // 2 + 1) * 16)
                    sp.sem_inc(q.passed, 1)

                each(sp, body)

            @block.gpsimd
            def _(pool):
                def body(n, block):
                    q.gather(pool, block, 0)
                    for j in range(CHUNKS):
                        q.low(pool, block, j, j % RING)
                    q.scatter(pool, block, 0)
                    q.release_y(pool, 0, n + NE // 2 + 1)

                each(pool, body)

            @block.scalar
            def _(act):
                def body(n, block):
                    q.move_x(act, block)
                    for j in range(CHUNKS):
                        q.high(act, block, j, j % RING, LOADS + (n * 2 + j // RING + 1 if j % RING < 2 else n + 1))
                    q.silu(act, block)
                    q.high_h(act, block)

                each(act, body)

            @block.vector
            def _(dve):
                def body(n, block):
                    q.move_x(dve, block)
                    for j in range(CHUNKS):
                        q.low(dve, block, j, j % RING)
                    q.multiply(dve, block)
                    q.low_h(dve, block)
                    q.move_y(dve, block, 0)

                each(dve, body)

            @block.tensor
            def _(pe):
                def body(n, block):
                    q.turn_x(pe, block, 0, n + NE // 2 + 1)
                    q.gate_up(pe, block)
                    q.turn_h(pe, block)
                    q.down(pe, block)

                each(pe, body)


def finish(nc, a, s):
    with ExitStack() as stack:
        t = Mem(nc, stack)
        yy = [t.sb(f"yy{b}", [P, 2, D]) for b in range(4)]
        junk = t.sb("junk6", [P, D])
        gain = t.sb("gain", [1, D])
        gains = t.sb("gains", [P, D])
        onerow, epsb = t.sb("onerow6", [1, P]), t.sb("epsb6", [P, 1])
        ss, root, rstd, tmp = (t.sb(n, [P, NT]) for n in ("ss6", "root6", "rstd6", "tmp6"))
        p_g = t.ps("p_g6", [P, 2, 512])
        y_in = [t.sem(f"y_in{b}") for b in range(4)]
        g_in, consts, spread, spread_ok = t.sem("g_in"), t.sem("consts6"), t.sem("spread"), t.sem("spread_ok")
        summed, squared, rooted, scaled, stored, chain = (t.sem(n) for n in ("summed6", "squared6", "rooted6", "scaled6", "stored", "chain6"))

        with nc.Block() as block:

            @block.sync
            def _(sp):
                sp.dma_start(gain[:], a.g_final).then_inc(g_in, 16)
                for i in range(NT):
                    if i >= 4:
                        sp.wait_ge(summed, 2 * (i - 3))
                    src = a.y_rows.rearrange("(c n) d -> n c d", c=2)[i * P:(i + 1) * P]
                    sp.dma_start(yy[i % 4][:], src).then_inc(y_in[i % 4], 16)

            @block.gpsimd
            def _(pool):
                pool.memset(onerow[:], 1.0).then_inc(consts, 1)
                pool.memset(epsb[:], EPS).then_inc(consts, 1)

            @block.tensor
            def _(pe):
                pe.wait_ge(consts, 2)
                pe.wait_ge(g_in, 16)
                for h in range(2):
                    last = pe.matmul(p_g[:, h, :], onerow[:], gain[:, h * 512:(h + 1) * 512], start=True, stop=True)
                last.then_inc(spread, 1)

            @block.scalar
            def _(act):
                act.wait_ge(spread, 1)
                act.activation(gains[:].rearrange("p (c n) -> p c n", c=2), p_g[:], ACT.Copy).then_inc(spread_ok, 1)
                act.wait_ge(consts, 2)
                for i in range(NT):
                    act.wait_ge(summed, 2 * (i + 1))
                    act.wait_ge(squared, i)
                    act.activation(junk[:], s.x1[:, i, :], ACT.Square, accum_out=ss[:, i:i + 1]).then_inc(squared, 1)
                    act.wait_ge(squared, i + 1)
                    act.activation(root[:, i:i + 1], ss[:, i:i + 1], ACT.Sqrt, scale=1.0 / D, bias=epsb[:, 0:1]).then_inc(rooted, 1)
                for i in range(NT):
                    act.wait_ge(scaled, i + 1)
                    act.dma_start(a.out[i * P:(i + 1) * P, :], s.x1[:, i, :]).then_inc(stored, 16)
                act.wait_ge(stored, 16 * NT)

            @block.vector
            def _(dve):
                c = Counter(dve, chain)

                def add(i):
                    dve.wait_ge(y_in[i % 4], 16 * (i // 4 + 1))
                    x1 = s.x1[:, i, :]
                    for k in range(2):
                        dve.tensor_tensor(x1, x1, yy[i % 4][:, k, :], ALU.add).then_inc(summed, 1)
                        if k == 0:
                            dve.wait_ge(summed, 2 * i + 1)

                def scale(i):
                    one = slice(i, i + 1)
                    dve.wait_ge(rooted, i + 1)
                    c.step(dve.reciprocal(rstd[:, one], root[:, one]))
                    newton(dve, c, rstd[:, one], ss[:, one], tmp[:, one], D, n=1)
                    dve.wait_ge(spread_ok, 1)
                    x1 = s.x1[:, i, :]
                    dve.scalar_tensor_tensor(x1, x1, rstd[:, one], gains[:], ALU.mult, ALU.mult).then_inc(scaled, 1)

                for i in range(NT):
                    add(i)
                    if i >= 1:
                        scale(i - 1)
                scale(NT - 1)


def build(nc, arrays, out):
    a = Arrays(arrays)
    a.out = out
    a.h_rows = nc.dram_tensor("h_rows", (N, D), F32).ap()
    a.y_rows = nc.dram_tensor("y_rows", (2 * N, D), F32).ap()
    a.slot_rows = nc.dram_tensor("slot_rows", (SLOTS, 4), I32).ap()
    a.v_rows = nc.dram_tensor("v_rows", (N, DN), F32).ap()
    with ExitStack() as stack:
        m = Mem(nc, stack)
        s = Buffers()
        s.ident = m.sb("ident", [P, P])
        s.ones = m.sb("ones", [P, P])
        s.vcol = m.sb("vcol", [P, a.vecs.shape[0]])
        s.cond = m.sb("cond", [P, 2 * KD])
        s.scale2 = m.sb("scale2", [P, KD])
        s.shift2 = m.sb("shift2", [P, KD])
        s.gate2 = m.sb("gate2", [P, D])
        s.blocks = m.sb("blocks", [1, OVB + 1], I32)
        s.x1 = m.sb("x1", [P, NT, D])
        s.loaded = [m.sem(f"loaded{r}") for r in range(RING)]
        s.raw = [m.sb(f"raw{r}", [P, CHUNK]) for r in range(RING)]
        with ExitStack() as mixer:
            mm = Mem(nc, mixer)
            s.ht = mm.sb("ht", [P, KD, N + L])
            s.vctx = mm.sb("vctx", [P, 2, DN])
            s.gate1 = mm.sb("gate1", [P, D])
            s.fout = mm.sb("fout", [P, NT, DF])
            norm_inputs(nc, mm, a, s)
            project_values(nc, mm, a, s)
            s.na = mm.sb("na", [P, NT, DN])
            attention(nc, mm, a, s)
            mix_and_route(nc, mm, a, s)
        s.act, s.pool = nc.scalar, nc.gpsimd
        experts(nc, a, s)
        finish(nc, a, s)


def query_order(x):
    g = x.reshape(2, QR, 4, QC, *x.shape[1:]).swapaxes(1, 2)
    return np.ascontiguousarray(g[:, :, ::-1, ::-1].reshape(x.shape))


def grid_order(x):
    g = x.reshape(2, 4, QR, QC, *x.shape[1:])[:, :, ::-1, ::-1].swapaxes(1, 2)
    return np.ascontiguousarray(g.reshape(x.shape))


def bf16_bits(x):
    return (x.view(np.uint32) >> 16).astype(np.uint16)


def shape_constants():
    c = {"ident": np.eye(P, dtype=np.float32)}
    w = HD
    ang = 2 * np.pi * (np.outer(np.arange(w), np.arange(w)) % w) / w
    norm = 1.0 / np.sqrt(N * w)
    c["chan"] = np.stack([np.kron(np.eye(2), f(ang) * norm) for f in (np.cos, np.sin)]).astype(np.float32)
    pos = query_order(np.arange(N))
    ang = 2 * np.pi * (np.outer(np.arange(N // 2), pos) % N) / N
    d = np.stack([np.cos(ang), -np.sin(ang)], axis=1)
    d[0, 1] = 1 - 2 * (pos % 2)
    d = d.reshape(N // 2, 2, NT, P)
    c["dft"] = np.ascontiguousarray(d.transpose(2, 0, 1, 3).astype(np.float32))
    half = HD // 4
    inv = 10000.0 ** (-np.arange(half, dtype=np.float32) / half)
    tok = np.arange(N)
    ch = np.arange(P) % HD
    where = np.where((ch < HD // 2)[:, None], (tok // GW)[None], (tok % GW)[None]).astype(np.float32)
    ang = where * inv[ch % half][:, None].astype(np.float32)
    c["rope"] = np.stack([np.cos(ang), np.sin(ang)]).astype(np.float32)
    rot = np.zeros((P, P), np.float32)
    for i in range(P):
        if i % (2 * half) < half:
            rot[i + half, i] = -1.0
        else:
            rot[i - half, i] = 1.0
    c["rot"] = rot
    mask = np.zeros((2, 4, P, KR, KC), np.float32)
    for h in range(2):
        for j in range(4):
            for p in range(P):
                r, q = QR * h + QR - 1 - p // QC, QC * j + QC - 1 - p % QC
                r0, c0 = min(max(r - 4, 0), 8), min(max(q - 8, 0), 48)
                kr, kc = 4 * h + np.arange(KR), COL0[j] + np.arange(KC)
                ok = ((kr >= r0) & (kr < r0 + 8))[:, None] & ((kc >= c0) & (kc < c0 + 16))[None]
                mask[h, j, p] = np.where(ok, 0.0, NEG)
    c["mask"] = bf16_bits(np.ascontiguousarray(mask.reshape(8, P, LOC).transpose(1, 0, 2)))
    c["before"] = np.triu(np.ones((P, P), np.float32), 1)
    c["desc"] = np.broadcast_to(np.arange(EPG, 0, -1, dtype=np.float32), (P, NT, EPG)).copy()
    c["base"] = np.broadcast_to(np.arange(NE, dtype=np.float32) * CAP, (P, NE)).copy()
    c["blk"] = np.broadcast_to(np.arange(OVB, dtype=np.float32)[:, None], (1, OVB, NE)).copy()
    tok = np.arange(N, dtype=np.int32).reshape(NT, P).T
    c["ids"] = np.stack([np.stack([tok, tok + k * N, 0 * tok, 0 * tok], axis=-1) for k in range(2)], axis=1).astype(np.int32)
    return c


def host_layout(x, c, ctx, c_ctx, w_ada, b_ada, g_norm1, w_in, w_fmix, rpb, g_out, w_out, g_norm2,
                w_router_group, w_router_expert, w_gate, w_up, w_down, g_final):
    h = {k: np.asarray(v) for k, v in dict(
        x=x, c=c, ctx=ctx, c_ctx=c_ctx, w_ada=w_ada, b_ada=b_ada, g_norm1=g_norm1, w_in=w_in, w_fmix=w_fmix, rpb=rpb,
        g_out=g_out, w_out=w_out, g_norm2=g_norm2, wrg=w_router_group, wre=w_router_expert, w_gate=w_gate,
        w_up=w_up, w_down=w_down, g_final=g_final).items()}
    out = shape_constants()
    out["vecs"] = np.concatenate([h[k].reshape(-1, P) for k in ("b_ada", "c", "c_ctx", "g_norm1", "g_norm2", "g_out")])
    out["x_nat"] = h["x"].reshape(N, D)
    out["x_perm"] = query_order(h["x"].reshape(N, D))
    out["ctx"] = h["ctx"].reshape(L, D)
    for k in ("w_ada", "w_in", "w_fmix", "w_out", "w_gate", "w_up", "w_down"):
        out[k] = h[k].reshape(h[k].shape[1:])
    out["b_ada"] = h["b_ada"]
    rows = np.zeros((NH, RPB), np.float32)
    body = np.zeros((NH, 15, PITCH), np.float32)
    body[:, :, 0:31] = h["rpb"][0]
    rows[:, LEAD:LEAD + 15 * PITCH] = body.reshape(NH, -1)
    out["rpb"] = rows
    out["w_router"] = np.concatenate([h["wrg"][0], h["wre"][0]], axis=1)
    out["g_final"] = h["g_final"].reshape(1, D)
    return out


def kernel(**inputs):
    import concourse.bacc as bacc
    from concourse.bass_utils import run_bass_kernel_spmd

    arrays = {f"in_{k}": v for k, v in host_layout(**inputs).items()}
    nc = bacc.Bacc("TRN2", target_bir_lowering=False, num_devices=1)
    aps = {k[3:]: nc.dram_tensor(k, v.shape, mybir.dt.from_np(v.dtype), kind="ExternalInput").ap() for k, v in arrays.items()}
    out = nc.dram_tensor("out", (N, D), F32, kind="ExternalOutput").ap()
    build(nc, aps, out)
    r = run_bass_kernel_spmd(nc, [arrays], core_ids=[0])
    return grid_order(r.results[0]["out"]).reshape(1, N, D)
```
